# Optimizing a Trainium2 kernel written in Bass

```python
import jax, jax.numpy as jnp
from jax import lax
import numpy as np

D_MODEL = 1024
BATCH = 1
SEQ = 1024
DEPTH = 1

N_HEADS = 8
HEAD_DIM = 64
ATTN_WIDTH = N_HEADS * HEAD_DIM
IDX_HEADS = 8
IDX_DIM = 64
INDEX_TOPK_MAX = 256
CONV_WIDTH = 512
CONV_GROUPS = 8
CONV_K = 3
N_BRANCHES = 2
D_FF = 2816
FFN_CONV_K = 3
Q_BLOCK = 64
EPS = 1e-6

kernel_name = "hybrid_gated_dsa_shortconv_convffn"

SPLIT_SIZES = (
    ATTN_WIDTH,
    ATTN_WIDTH,
    ATTN_WIDTH,
    IDX_HEADS * IDX_DIM,
    IDX_DIM,
    IDX_HEADS,
    CONV_WIDTH,
    CONV_WIDTH,
    CONV_WIDTH,
    N_BRANCHES * D_MODEL,
)
IN_COLS = sum(SPLIT_SIZES)

def rms_norm(x, g):
    xf = x.astype(jnp.float32)
    y = xf * lax.rsqrt(jnp.mean(xf * xf, axis=-1, keepdims=True) + EPS)
    return (y * g.astype(jnp.float32)).astype(x.dtype)

def causal_dwconv(u, w):
    ksz = w.shape[0]
    s = u.shape[1]
    up = jnp.pad(u, ((0, 0), (ksz - 1, 0), (0, 0)))
    y = up[:, 0:s] * w[0]
    for j in range(1, ksz):
        y = y + up[:, j:j + s] * w[j]
    return y

def sparse_attention(q, k, v, iq, ik, iw):
    b, s = q.shape[0], q.shape[1]
    topk = min(INDEX_TOPK_MAX, s // 4)
    nb = s // Q_BLOCK
    scale = HEAD_DIM ** -0.5
    iw = iw.astype(jnp.float32) * (IDX_HEADS ** -0.5) * (IDX_DIM ** -0.5)
    ikf = ik.astype(jnp.float32)
    key_pos = jnp.arange(s)

    def to_blocks(a):
        return a.reshape((b, nb, Q_BLOCK) + a.shape[2:]).swapaxes(0, 1)

    starts = jnp.arange(nb) * Q_BLOCK

    def block(args):
        qb, iqb, iwb, start = args
        qpos = start + jnp.arange(Q_BLOCK)
        causal = key_pos[None, :] <= qpos[:, None]
        dots = jnp.einsum('bqhd,bsd->bqhs', iqb.astype(jnp.float32), ikf)
        score = jnp.einsum('bqhs,bqh->bqs', jax.nn.relu(dots), iwb)
        score = jnp.where(causal[None], score, -jnp.inf)
        top_val, top_idx = lax.top_k(score, topk)
        valid = jnp.isfinite(top_val)
        k_sel = jax.vmap(lambda kb, ib: kb[ib])(k, top_idx)
        v_sel = jax.vmap(lambda vb, ib: vb[ib])(v, top_idx)
        logits = jnp.einsum('bqhd,bqkhd->bqhk', qb, k_sel).astype(jnp.float32) * scale
        logits = jnp.where(valid[:, :, None, :], logits, -jnp.inf)
        p = jax.nn.softmax(logits, axis=-1).astype(v.dtype)
        return jnp.einsum('bqhk,bqkhd->bqhd', p, v_sel)

    out = lax.map(block, (to_blocks(q), to_blocks(iq), to_blocks(iw), starts))
    return out.swapaxes(0, 1).reshape(b, s, N_HEADS * HEAD_DIM)

def setup_inputs(seed: int = 0) -> dict:
    key = jax.random.key(seed)
    ks = jax.random.split(key, 16)
    f32 = jnp.float32

    def nrm(k, shape, scale):
        return jax.random.normal(k, shape, f32) * scale

    return {
        "x": jax.random.normal(ks[0], (BATCH, SEQ, D_MODEL), f32),
        "norm_mix_g": 1.0 + nrm(ks[1], (DEPTH, D_MODEL), 0.02),
        "w_in": nrm(ks[2], (DEPTH, D_MODEL, IN_COLS), D_MODEL ** -0.5),
        "b_gate": nrm(ks[3], (DEPTH, N_BRANCHES * D_MODEL), 0.02),
        "w_attn_out": nrm(ks[4], (DEPTH, ATTN_WIDTH, D_MODEL), ATTN_WIDTH ** -0.5),
        "conv_w": nrm(ks[5], (DEPTH, CONV_K, CONV_WIDTH), CONV_K ** -0.5),
        "w_conv_out": nrm(ks[6], (DEPTH, CONV_WIDTH, D_MODEL), CONV_WIDTH ** -0.5),
        "w_o": nrm(ks[7], (DEPTH, D_MODEL, D_MODEL), D_MODEL ** -0.5),
        "norm_ffn_g": 1.0 + nrm(ks[8], (DEPTH, D_MODEL), 0.02),
        "w_up": nrm(ks[9], (DEPTH, D_MODEL, 2 * D_FF), D_MODEL ** -0.5),
        "ffn_conv_w": nrm(ks[10], (DEPTH, FFN_CONV_K, 2 * D_FF), FFN_CONV_K ** -0.5),
        "w_down": nrm(ks[11], (DEPTH, D_FF, D_MODEL), D_FF ** -0.5),
        "norm_final_g": 1.0 + nrm(ks[12], (D_MODEL,), 0.02),
    }

def reference(x, norm_mix_g, w_in, b_gate, w_attn_out, conv_w, w_conv_out, w_o,
              norm_ffn_g, w_up, ffn_conv_w, w_down, norm_final_g):
    b, s, _ = x.shape
    split_points = list(np.cumsum(SPLIT_SIZES)[:-1])
    h = x
    for l in range(DEPTH):
        xn = rms_norm(h, norm_mix_g[l])
        proj = jnp.einsum('bsd,dc->bsc', xn, w_in[l])
        q, k, v, iq, ik, iw, ch, cb, cc, gates = jnp.split(proj, split_points, axis=-1)
        q = q.reshape(b, s, N_HEADS, HEAD_DIM)
        k = k.reshape(b, s, N_HEADS, HEAD_DIM)
        v = v.reshape(b, s, N_HEADS, HEAD_DIM)
        iq = iq.reshape(b, s, IDX_HEADS, IDX_DIM)
        attn = sparse_attention(q, k, v, iq, ik, iw)
        branch_a = jnp.einsum('bsc,cd->bsd', attn, w_attn_out[l])
        conv = causal_dwconv(cc * ch, conv_w[l])
        branch_c = jnp.einsum('bsc,cd->bsd', cb * conv, w_conv_out[l])
        g = jax.nn.sigmoid(gates + b_gate[l])
        g_a, g_c = jnp.split(g, N_BRANCHES, axis=-1)
        merged = g_a * branch_a + g_c * branch_c
        h = h + jnp.einsum('bsd,de->bse', merged, w_o[l])
        xn2 = rms_norm(h, norm_ffn_g[l])
        up = jnp.einsum('bsd,df->bsf', xn2, w_up[l])
        up = causal_dwconv(up, ffn_conv_w[l])
        gt, val = jnp.split(up, 2, axis=-1)
        h = h + jnp.einsum('bsf,fd->bsd', jax.nn.silu(gt) * val, w_down[l])
    return rms_norm(h, norm_final_g)


_drawn_inputs = setup_inputs


def setup_inputs(seed=0):
    import zlib

    import numpy as np

    out = dict(_drawn_inputs(seed))
    spreads = {}
    factors = {'b_gate': 8.0, 'norm_ffn_g': 4.434, 'norm_final_g': 2.894}
    for name, (base, spread) in spreads.items():
        noise = np.random.default_rng([zlib.crc32(name.encode()), seed]).standard_normal(out[name].shape)
        drawn = base * np.exp(spread * noise) if base else spread * noise
        out[name] = __import__('jax').numpy.asarray(drawn.astype(out[name].dtype))
    for name, factor in factors.items():
        out[name] = (out[name] * factor).astype(out[name].dtype)
    return out
```

```python
from contextlib import ExitStack, contextmanager

import numpy as np

import concourse.bass as bass
from concourse import mybir

P = 128
D = 1024
S = 1024
DT = D // P
ST = S // P
NH = 8
HD = 64
PT_ = NH * HD // P
CW = 512
CT = CW // P
FF = 2816
FT = FF // P
TOPK = 256
EPS = 1e-6
HALF = 512

Q0, K0, V0 = 0, 512, 1024
IQ0, IK0, IW0 = 1536, 2048, 2112
CH0, CB0, CC0, G0 = 2120, 2632, 3144, 3656

C_IKW = 0
C_IQ = 1
C_CONV = 5
C_GROUP = 17
C_Q = 29
C_K = 33
C_V = 37
C_GA = 41
C_AO = 49
C_WO = 53
C_FF = 61
N_CHUNKS = 127

T_GMIX, T_GFFN, T_GFIN, T_BIAS = 0, 8, 16, 24
T_CONV = 40
T_FCONV = T_CONV + 3 * CT
N_CONST = T_FCONV + 3 * 2 * FT

TAKEN = -3e38
ACAUSAL = -1e38
UNCHOSEN = -2e38
MASKED = -1e30


def mask_at(t):
    return P * t * (t + 1) // 2


def tickets():
    order = ["n0_sum", "n0_bc", "ikw", *[("iq", p) for p in range(PT_)], "iw_tok"]
    order += [("dots", t, h) for t in range(2, ST) for h in range(NH)]
    order += [("conv", n) for n in range(3 * CT)]
    for j in range(4):
        order += [("gc", 2 * j), ("gc", 2 * j + 1), ("co", 2 * j), ("co", 2 * j + 1)]
    order += [("q", p) for p in range(PT_)] + [("k", p) for p in range(PT_)]
    order += [("v", 0)]
    for p in range(1, PT_):
        order += [("v", p), ("vt", p - 1)]
    order += [("ga", 0), ("vt", PT_ - 1)] + [("ga", e) for e in range(1, DT)]
    units = ST * NH
    order += [("s", 0), ("s", 1)]
    for u in range(units + 1):
        if u < units:
            order += [("pt", u)]
        if u + 2 < units:
            order += [("s", u + 2)]
        if u >= 1 and (u - 1) % 2:
            order += [("o", (u - 1) // 2)]
    order += [("ao", e) for e in range(DT)] + [("wo", e) for e in range(DT)]
    order += ["n1_sum", "n1_bc"]
    order += [("up", 0, m) for m in range(4)]
    for g in range(1, FT // 2):
        order += [("up", g, m) for m in range(4)] + [("dn", g - 1, e) for e in range(DT)]
    order += [("dn", FT // 2 - 1, e) for e in range(DT)]
    order += ["n2_sum", "n2_bc"]
    return {name: n for n, name in enumerate(order)}


def build(nc, xT, wts, consts, outT, bc_dram, ga_dram):
    f32, f32r = mybir.dt.float32, mybir.dt.float32r
    ALU, ACT = mybir.AluOpType, mybir.ActivationFunctionType
    ds = bass.ds
    U = tickets()
    units = ST * NH
    scale = float(HD) ** -0.5
    iw_scale = float(NH) ** -0.5 * float(HD) ** -0.5

    KB = 1024
    base = 16512
    X = base
    Q = X + 64 * KB
    M = Q + 80 * KB
    W = M + 18 * KB
    G = W + 28 * KB
    Z = G + 8 * KB

    def at(name, shape, dt, where):
        return nc.alloc_sbuf_tensor_at(name, [P, *shape], dt, offset=where)

    w_raw = at("w_raw", [3, 8, P], f32, W)
    w_hi = at("w_hi", [2, 8, P], f32r, W + 12 * KB)
    w_lo = at("w_lo", [2, 8, P], f32r, W + 20 * KB)
    stage = at("stage", [2, S], f32, G)
    const = at("const", [N_CONST], f32, Z)
    ident = at("ident", [P], f32, Z + 1024)
    ones = at("ones", [P], f32, Z + 1536)
    small = at("small", [64], f32, Z + 2048)
    iw_tok = at("iw_tok", [ST, NH], f32, Z + 2304)
    att_small = at("att_small", [4, 4], f32, Z + 2560)
    top8 = at("top8", [8], f32, Z + 2624)

    xn_hi = at("xn_hi", [DT, S], f32r, X)
    xn_lo = at("xn_lo", [DT, S], f32r, X + 32 * KB)
    x_in = at("x_in", [DT, S], f32, Q)
    nrm_acc = at("nrm_acc", [S], f32, Q + 64 * KB)
    nrm_diag = at("nrm_diag", [ST, P], f32, Q + 68 * KB)
    nrm_x = at("nrm_x", [2, S], f32, Q + 72 * KB)
    iq_hi = at("iq_hi", [PT_, S], f32r, Q)
    iq_lo = at("iq_lo", [PT_, S], f32r, Q + 16 * KB)
    ik_hi = at("ik_hi", [S], f32r, Q + 32 * KB)
    ik_lo = at("ik_lo", [S], f32r, Q + 36 * KB)
    rel = at("rel", [2, S], f32, Q + 40 * KB)
    conv_h = at("conv_h", [CT, S], f32, Q)
    conv_c = at("conv_c", [CT, S], f32, Q + 16 * KB)
    conv_b = at("conv_b", [CT, S], f32, Q + 32 * KB)
    cv_hi = at("cv_hi", [CT, S], f32r, Q + 48 * KB)
    cv_lo = at("cv_lo", [CT, S], f32r, Q + 64 * KB)
    q_raw = at("q_raw", [PT_, S], f32, Q)
    k_hi = at("k_hi", [PT_, S], f32r, Q + 16 * KB)
    k_lo = at("k_lo", [PT_, S], f32r, Q + 32 * KB)
    v_hi = at("v_hi", [ST, NH * HD], f32r, Q + 48 * KB)
    v_lo = at("v_lo", [ST, NH * HD], f32r, Q + 64 * KB)
    mask = at("mask", [ST * (ST + 1) // 2 * P], f32, M)
    probs = at("probs", [2, S], f32, X)
    pt_hi = at("pt_hi", [2, S], f32r, X + 8 * KB)
    pt_lo = at("pt_lo", [2, S], f32r, X + 16 * KB)
    qs_hi = at("qs_hi", [2, PT_, P], f32r, X + 24 * KB)
    qs_lo = at("qs_lo", [2, PT_, P], f32r, X + 28 * KB)
    at_hi = at("at_hi", [PT_, S], f32r, X + 32 * KB)
    at_lo = at("at_lo", [PT_, S], f32r, X + 48 * KB)
    gate_in = at("gate_in", [2, 2, S], f32, M)
    mg_hi = at("mg_hi", [DT, S], f32r, Q)
    mg_lo = at("mg_lo", [DT, S], f32r, Q + 32 * KB)
    h = at("h", [DT, S], f32, X)
    xm_hi = at("xm_hi", [DT, S], f32r, Q)
    xm_lo = at("xm_lo", [DT, S], f32r, Q + 32 * KB)
    ff_t = at("ff_t", [4, S], f32, M)
    u_hi = at("u_hi", [2, 2, S], f32r, X + 32 * KB)
    u_lo = at("u_lo", [2, 2, S], f32r, X + 48 * KB)

    ctx = ExitStack()
    with ctx:
        pair = [ctx.enter_context(nc.psum_tensor(f"pair{i}", [P, S], f32)) for i in range(4)]

        def sem(name):
            return ctx.enter_context(nc.semaphore(name))

        const_in = sem("const_in")
        x_loaded = [sem(f"x_loaded{d}") for d in range(DT)]
        w_loaded = [sem(f"w_loaded{s}") for s in range(3)]
        w_hi_done, w_lo_done = sem("w_hi_done"), sem("w_lo_done")
        out_ready = sem("out_ready")
        evacuated = [sem(f"evacuated{i}") for i in range(4)]
        fixed_ready, ident_zero = sem("fixed_ready"), sem("ident_zero")
        square_done, acc_done, newton = sem("square_done"), sem("acc_done"), sem("newton")
        var_done, sqrt_done, diag_done = sem("var_done"), sem("sqrt_done"), sem("diag_done")
        scaled_done, norm_hi, norm_lo = sem("scaled_done"), sem("norm_hi"), sem("norm_lo")
        ik_hi_done, iw_copied = sem("ik_hi_done"), sem("iw_copied")
        ik_copied = [sem("ik_hi_copied"), sem("ik_lo_copied")]
        iq_hi_done = sem("iq_hi_done")
        score_step, causal_done = sem("score_step"), sem("causal_done")
        topk_step, mask_done = sem("topk_step"), sem("mask_done")
        conv_step, conv_hi_done, conv_lo_done = sem("conv_step"), sem("conv_hi_done"), sem("conv_lo_done")
        gc_done, co_copied, bc_done = sem("gc_done"), sem("co_copied"), sem("bc_done")
        bc_stored = [sem("bc_stored0"), sem("bc_stored1")]
        ga_stored = [sem("ga_stored0"), sem("ga_stored1")]
        k_staged, k_lo_done, v_staged, v_lo_done = sem("k_staged"), sem("k_lo_done"), sem("v_staged"), sem("v_lo_done")
        qs_hi_done, qs_lo_done = sem("qs_hi_done"), sem("qs_lo_done")
        negmax_done, exp_done, recip_done, probs_done = (
            sem("negmax_done"), sem("exp_done"), sem("recip_done"), sem("probs_done"))
        pt_hi_done, pv_even_done, o_hi_done = sem("pt_hi_done"), sem("pv_even_done"), sem("o_hi_done")
        gate_loaded = [sem("gate_loaded0"), sem("gate_loaded1")]
        merged, mg_hi_done, mg_lo_done = sem("merged"), sem("mg_hi_done"), sem("mg_lo_done")
        tap2_done, tap1_done = sem("tap2_done"), sem("tap1_done")
        silu_done, ff_done, u_hi_done, u_lo_done = sem("silu_done"), sem("ff_done"), sem("u_hi_done"), sem("u_lo_done")
        out_scaled = sem("out_scaled")
        out_stored = [sem("out_stored0"), sem("out_stored1")]

        block = ctx.enter_context(nc.Block())

        def wait_output(eng, name, more=0):
            eng.wait_ge(out_ready, U[name] + 1 + more)

        def wait_evacuated(eng, name, laps=0):
            eng.wait_ge(evacuated[U[name] % 4], U[name] // 4 + 1 + laps)

        def psum(name):
            return pair[U[name] % 4]

        def freed(name):
            return evacuated[U[name] % 4]

        last_of = [("ikw")] + [("iq", p) for p in range(PT_)] + [("conv", n) for n in range(12)]
        for j in range(4):
            last_of += [("gc", 2 * j), ("gc", 2 * j + 1), ("co", 2 * j + 1)]
        last_of += [("q", p) for p in range(4)] + [("k", p) for p in range(4)] + [("v", p) for p in range(4)]
        last_of += [("ga", e) for e in range(8)] + [("ao", 2 * j + 1) for j in range(4)] + [("wo", e) for e in range(8)]
        last_of += [("up", 0, m) for m in range(4)]
        for g in range(1, FT // 2):
            last_of += [("up", g, m) for m in range(4)] + [("dn", g - 1, 3), ("dn", g - 1, 7)]
        last_of += [("dn", FT // 2 - 1, 3), ("dn", FT // 2 - 1, 7)]
        assert len(last_of) == N_CHUNKS

        @block.sync
        def _(sp):
            def load_chunk(c, lap=None):
                if c >= 3:
                    sp.wait_ge(w_lo_done, c - 2 + (0 if lap is None else 12 * lap))
                src = wts[c] if lap is None else wts[ds(c + 12 * lap, 1)].rearrange("a p n -> p (a n)")
                sp.dma_start(w_raw[:, c % 3].rearrange("p a b -> p (a b)"), src).then_inc(w_loaded[c % 3], 16)

            sp.dma_start(const[:], consts).then_inc(const_in, 16)
            for d in range(DT):
                sp.dma_start(x_in[:, d], xT[d]).then_inc(x_loaded[d], 16)
            for c in range(C_AO + 5):
                load_chunk(c)
                j, at_end = divmod(c - (C_GROUP + 2 + 5), 3)
                if at_end == 0 and 0 <= j < 4:
                    for e in (2 * j, 2 * j + 1):
                        sp.wait_ge(bc_done, e + 1)
                        sp.dma_start(bc_dram[e], conv_c[:, 2 + e % 2]).then_inc(bc_stored[e % 2], 16)
                e = c - (C_GA + 5)
                if 0 <= e < DT:
                    wait_evacuated(sp, ("ga", e))
                    sp.dma_start(ga_dram[e], stage[:, e % 2]).then_inc(ga_stored[e % 2], 16)
            wait_evacuated(sp, ("s", units - 1))
            for n in range(2):
                sp.wait_ge(bc_stored[n], 16 * DT // 2)
                sp.wait_ge(ga_stored[n], 16 * DT // 2)
            for e in range(DT):
                if e >= 2:
                    sp.wait_ge(merged, e - 1)
                sp.dma_start(gate_in[:, e % 2, 0], ga_dram[e]).then_inc(gate_loaded[e % 2], 16)
                sp.dma_start(gate_in[:, e % 2, 1], bc_dram[e]).then_inc(gate_loaded[e % 2], 16)
                if e == 1:
                    wait_evacuated(sp, ("o", units // 2 - 1))
                    for d in range(DT):
                        sp.dma_start(h[:, d], xT[d]).then_inc(x_loaded[d], 16)
            for c in range(C_AO + 5, C_FF + 6):
                load_chunk(c)
            with sp.Fori(0, 5) as i:
                for n in range(12):
                    load_chunk(C_FF + 6 + n, i)
            for d in range(DT):
                sp.wait_ge(out_scaled, d + 1)
                sp.dma_start(outT[d], nrm_x[:, d % 2]).then_inc(out_stored[d % 2], 16)
            for n in range(2):
                sp.wait_ge(out_stored[n], 16 * DT // 2)

        @block.tensor
        def _(pe):
            def take_pair(name, more=0, laps=0):
                if U[name] >= 4:
                    pe.wait_ge(evacuated[U[name] % 4], U[name] // 4 + laps)

            def three(out, w_h, w_l, x_h, x_l, first, last):
                nc.tensor.matmul(out, w_h, x_h, start=first, stop=False)
                nc.tensor.matmul(out, w_h, x_l, start=False, stop=False)
                return nc.tensor.matmul(out, w_l, x_h, start=False, stop=last)

            def product(name, slot, blocks, x_h, x_l, each_k=None):
                for half in range(2):
                    cols = slice(half * HALF, (half + 1) * HALF)
                    for n, b in enumerate(blocks):
                        if each_k is not None and half == 0:
                            each_k(n)
                        last = three(psum(name)[:, cols], w_hi[:, slot, b], w_lo[:, slot, b],
                                     x_h(n)[:, cols], x_l(n)[:, cols], n == 0, n == len(blocks) - 1)
                last.then_inc(out_ready, 1)

            def chunk(c, names, x_h, x_l, each_k=None, lap=None, laps_psum=0):
                pe.wait_ge(w_lo_done, c + 1 + (0 if lap is None else 12 * lap))
                per = 8 // len(names)
                for n, name in enumerate(names):
                    take_pair(name, laps=laps_psum)
                    product(name, c % 2, range(n * per, (n + 1) * per), x_h, x_l, each_k)

            def norm(n):
                a, b = f"n{n}_sum", f"n{n}_bc"
                take_pair(a)
                if n == 0:
                    pe.wait_ge(fixed_ready, 3)
                pe.wait_ge(acc_done, DT * (n + 1))
                for t in range(ST):
                    last = nc.tensor.matmul(psum(a)[:, t:t + 1], nrm_acc[:, t * P:(t + 1) * P], ones[:, 0:1],
                                            start=True, stop=True)
                last.then_inc(out_ready, 1)
                take_pair(b)
                pe.wait_ge(diag_done, n + 1)
                for half in range(2):
                    last = nc.tensor.matmul(psum(b)[:, half * HALF:(half + 1) * HALF], ones[:],
                                            nrm_diag[:, 4 * half:4 * half + 4].rearrange("p a b -> p (a b)"),
                                            start=True, stop=True)
                last.then_inc(out_ready, 1)

            def from_xn():
                return (lambda k: xn_hi[:, k]), (lambda k: xn_lo[:, k])

            norm(0)
            chunk(C_IKW, ["ikw"], *from_xn(), each_k=lambda k: pe.wait_ge(norm_lo, k + 1))
            for p in range(PT_):
                chunk(C_IQ + p, [("iq", p)], *from_xn())
            take_pair("iw_tok")
            pe.wait_ge(iw_copied, 1)
            for t in range(ST):
                last = nc.tensor.transpose(psum("iw_tok")[:, t * NH:(t + 1) * NH],
                                           stage[HD:HD + NH, 0, t * P:(t + 1) * P], ident[HD:HD + NH, HD:HD + NH])
            last.then_inc(out_ready, 1)
            for s in ik_copied:
                pe.wait_ge(s, 16)
            for t in range(2, ST):
                for hh in range(NH):
                    name = ("dots", t, hh)
                    p, r = hh // 2, slice(HD * (hh % 2), HD * (hh % 2) + HD)
                    take_pair(name)
                    wait_evacuated(pe, ("iq", p))
                    for k0 in range(0, (t + 1) * P, HALF):
                        cols = slice(k0, min(k0 + HALF, (t + 1) * P))
                        q = slice(t * P, (t + 1) * P)
                        last = three(psum(name)[:, cols], iq_hi[r, p, q], iq_lo[r, p, q],
                                     ik_hi[r, cols], ik_lo[r, cols], True, True)
                    last.then_inc(out_ready, 1)
            for n in range(3 * CT):
                chunk(C_CONV + n, [("conv", n)], *from_xn())
            for j in range(4):
                chunk(C_GROUP + 3 * j, [("gc", 2 * j)], *from_xn())
                chunk(C_GROUP + 3 * j + 1, [("gc", 2 * j + 1)], *from_xn())
                if j == 0:
                    pe.wait_ge(conv_lo_done, CT)
                chunk(C_GROUP + 3 * j + 2, [("co", 2 * j), ("co", 2 * j + 1)],
                      lambda k: cv_hi[:, k], lambda k: cv_lo[:, k])
            for p in range(PT_):
                chunk(C_Q + p, [("q", p)], *from_xn())
            for p in range(PT_):
                chunk(C_K + p, [("k", p)], *from_xn())

            def v_transposes(p):
                take_pair(("vt", p))
                wait_evacuated(pe, ("v", p))
                for t in range(ST):
                    last = nc.tensor.transpose(psum(("vt", p))[:, t * P:(t + 1) * P],
                                               stage[:, 0, t * P:(t + 1) * P], ident[:])
                last.then_inc(out_ready, 1)

            for p in range(PT_):
                chunk(C_V + p, [("v", p)], *from_xn())
                if p:
                    v_transposes(p - 1)
            chunk(C_GA, [("ga", 0)], *from_xn())
            v_transposes(PT_ - 1)
            for e in range(1, DT):
                chunk(C_GA + e, [("ga", e)], *from_xn())

            def logits(u):
                t, hh = divmod(u, NH)
                p, r = hh // 2, slice(HD * (hh % 2), HD * (hh % 2) + HD)
                name = ("s", u)
                take_pair(name)
                pe.wait_ge(qs_lo_done, t + 1)
                for k0 in range(0, (t + 1) * P, HALF):
                    cols = slice(k0, min(k0 + HALF, (t + 1) * P))
                    last = three(psum(name)[:, cols], qs_hi[r, t % 2, p], qs_lo[r, t % 2, p],
                                 k_hi[r, p, cols], k_lo[r, p, cols], True, True)
                last.then_inc(out_ready, 1)

            def transpose_probs(u):
                name = ("pt", u)
                take_pair(name)
                pe.wait_ge(probs_done, u + 1)
                for kb in range(u // NH + 1):
                    last = nc.tensor.transpose(psum(name)[:, kb * P:(kb + 1) * P],
                                               probs[:, u % 2, kb * P:(kb + 1) * P], ident[:])
                last.then_inc(out_ready, 1)

            def probs_times_v(u):
                t, hh = divmod(u, NH)
                p = hh // 2
                name = ("o", u // 2)
                if u % 2 == 0:
                    take_pair(name)
                wait_evacuated(pe, ("pt", u))
                out = psum(name)[:, (u % 2) * P:(u % 2 + 1) * P]
                for kb in range(t + 1):
                    last = three(out, v_hi[:, kb, p * P:(p + 1) * P], v_lo[:, kb, p * P:(p + 1) * P],
                                 pt_hi[:, u % 2, kb * P:(kb + 1) * P], pt_lo[:, u % 2, kb * P:(kb + 1) * P],
                                 kb == 0, kb == t)
                last.then_inc(out_ready if u % 2 else pv_even_done, 1)

            pe.wait_ge(k_lo_done, PT_)
            pe.wait_ge(v_lo_done, PT_)
            logits(0)
            logits(1)
            for u in range(units + 1):
                if u < units:
                    transpose_probs(u)
                if u + 2 < units:
                    logits(u + 2)
                if u >= 1:
                    probs_times_v(u - 1)

            wait_evacuated(pe, ("o", units // 2 - 1))
            for j in range(4):
                chunk(C_AO + j, [("ao", 2 * j), ("ao", 2 * j + 1)], lambda k: at_hi[:, k], lambda k: at_lo[:, k])
            for e in range(DT):
                chunk(C_WO + e, [("wo", e)], lambda k: mg_hi[:, k], lambda k: mg_lo[:, k],
                      each_k=(lambda k: pe.wait_ge(mg_lo_done, k + 1)) if e == 0 else None)
            norm(1)

            def up(g, c, more=None, laps=0):
                for m in range(4):
                    chunk(c + m, [("up", g, m)], lambda k: xm_hi[:, k], lambda k: xm_lo[:, k],
                          each_k=(lambda k: pe.wait_ge(norm_lo, DT + k + 1)) if g == 0 and m == 0 else None,
                          lap=more, laps_psum=laps)

            def down(g, c, more=None, laps=0):
                pe.wait_ge(u_lo_done, 2 * g + 2 + (0 if more is None else 4 * more))
                for n in range(2):
                    chunk(c + n, [("dn", g, 4 * n + e) for e in range(4)],
                          lambda k: u_hi[:, g % 2, k], lambda k: u_lo[:, g % 2, k], lap=more, laps_psum=laps)

            up(0, C_FF)
            with pe.Fori(0, 5) as i:
                for n in range(2):
                    up(1 + n, C_FF + 4 + 6 * n, i, 6 * i)
                    down(n, C_FF + 8 + 6 * n, i, 6 * i)
            down(FT // 2 - 1, N_CHUNKS - 2)
            norm(2)

        @block.scalar
        def _(act):
            A = nc.scalar

            def split(c, lap=None):
                act.wait_ge(w_loaded[c % 3], 16 * (c // 3 + 1) + (0 if lap is None else 64 * lap))
                if c >= 2:
                    wait_output(act, last_of[c - 2], 0 if lap is None else 24 * lap)
                A.copy(w_hi[:, c % 2], w_raw[:, c % 3]).then_inc(w_hi_done, 1)

            def norm(n, src, arrived):
                for d in range(DT):
                    arrived(d)
                    if DT * n + d >= 2:
                        act.wait_ge(acc_done, DT * n + d - 1)
                    A.activation(stage[:, d % 2], src[:, d], ACT.Square).then_inc(square_done, 1)
                act.wait_ge(var_done, n + 1)
                A.activation(small[:, 8:16], small[:, 0:8], ACT.Sqrt).then_inc(sqrt_done, 1)

            def norm_split(n, hi):
                for d in range(DT):
                    act.wait_ge(scaled_done, DT * n + d + 1)
                    A.copy(hi[:, d], nrm_x[:, d % 2]).then_inc(norm_hi, 1)

            def after(c):
                split(c + 2)

            norm(0, x_in, lambda d: act.wait_ge(x_loaded[d], 16))
            split(0)
            split(1)
            norm_split(0, xn_hi)
            wait_output(act, "ikw")
            A.copy(ik_hi[0:HD], psum("ikw")[0:HD]).then_inc(ik_hi_done, 1)
            A.mul(stage[HD:HD + NH, 0], psum("ikw")[HD:HD + NH], iw_scale).then_inc(iw_copied, 1)
            after(C_IKW)
            act.wait_ge(ik_hi_done, 1)
            act.dma_start(ik_hi[HD:P].bitcast(f32), ik_hi[0:HD].bitcast(f32)).then_inc(ik_copied[0], 16)
            wait_evacuated(act, "ikw")
            act.dma_start(ik_lo[HD:P].bitcast(f32), ik_lo[0:HD].bitcast(f32)).then_inc(ik_copied[1], 16)
            for p in range(PT_):
                wait_output(act, ("iq", p))
                A.copy(iq_hi[:, p], psum(("iq", p))[:]).then_inc(iq_hi_done, 1)
                after(C_IQ + p)
            n_dots = 0
            for t in range(2, ST):
                for hh in range(NH):
                    name, n = ("dots", t, hh), (t + 1) * P
                    wait_output(act, name)
                    if n_dots >= 2:
                        act.wait_ge(score_step, n_dots - 1)
                    A.activation(rel[:, n_dots % 2, 0:n], psum(name)[:, 0:n], ACT.Relu).then_inc(freed(name), 1)
                    n_dots += 1
            for n in range(3 * CT):
                p, which = divmod(n, 3)
                wait_output(act, ("conv", n))
                if n == 0:
                    act.wait_ge(score_step, n_dots)
                A.copy((conv_h, conv_c, conv_b)[which][:, p], psum(("conv", n))[:]).then_inc(freed(("conv", n)), 1)
                after(C_CONV + n)
            for j in range(4):
                for n in range(2):
                    e = 2 * j + n
                    wait_output(act, ("gc", e))
                    if e < 2:
                        act.wait_ge(conv_step, 5 * e + 4)
                    if e >= 2:
                        act.wait_ge(bc_done, e - 1)
                    A.activation(conv_c[:, n], psum(("gc", e))[:], ACT.Sigmoid,
                                 bias=const[:, T_BIAS + DT + e:T_BIAS + DT + e + 1]).then_inc(freed(("gc", e)), 1)
                    after(C_GROUP + 3 * j + n)
                    if j == 0 and n == 1:
                        for p in range(CT):
                            act.wait_ge(conv_step, 5 * (p + 1))
                            A.copy(cv_hi[:, p], conv_b[:, p]).then_inc(conv_hi_done, 1)
                for n in range(2):
                    e = 2 * j + n
                    wait_output(act, ("co", e))
                    if e >= 2:
                        act.wait_ge(bc_stored[e % 2], 16 * (e // 2))
                    A.copy(conv_c[:, 2 + n], psum(("co", e))[:]).then_inc(freed(("co", e)), 1)
                after(C_GROUP + 3 * j + 2)
            for p in range(PT_):
                wait_output(act, ("q", p))
                if p == 0:
                    for n in range(2):
                        act.wait_ge(bc_stored[n], 16 * DT // 2)
                A.copy(q_raw[:, p], psum(("q", p))[:]).then_inc(freed(("q", p)), 1)
                after(C_Q + p)
            for p in range(PT_):
                wait_output(act, ("k", p))
                if p >= 2:
                    act.wait_ge(k_lo_done, p - 1)
                A.copy(stage[:, p % 2], psum(("k", p))[:]).then_inc(k_staged, 1)
                A.copy(k_hi[:, p], psum(("k", p))[:]).then_inc(freed(("k", p)), 1)
                after(C_K + p)

            def v_split(p):
                wait_output(act, ("vt", p))
                src = psum(("vt", p))[:].rearrange("p (t c) -> p t c", c=P)
                if p:
                    act.wait_ge(v_lo_done, p)
                A.copy(stage[:, 1], psum(("vt", p))[:]).then_inc(v_staged, 1)
                A.copy(v_hi[:, :, p * P:(p + 1) * P], src).then_inc(freed(("vt", p)), 1)

            for p in range(PT_):
                wait_output(act, ("v", p))
                if p == 0:
                    act.wait_ge(k_lo_done, PT_)
                else:
                    wait_output(act, ("vt", p - 1))
                A.copy(stage[:, 0], psum(("v", p))[:]).then_inc(freed(("v", p)), 1)
                after(C_V + p)
                if p:
                    v_split(p - 1)
            for e in range(DT):
                if e == 1:
                    v_split(PT_ - 1)
                    act.wait_ge(v_lo_done, PT_)
                wait_output(act, ("ga", e))
                if e == 0:
                    wait_output(act, ("vt", PT_ - 1))
                if e >= 2:
                    act.wait_ge(ga_stored[e % 2], 16 * (e // 2))
                A.activation(stage[:, e % 2], psum(("ga", e))[:], ACT.Sigmoid,
                             bias=const[:, T_BIAS + e:T_BIAS + e + 1]).then_inc(freed(("ga", e)), 1)
                after(C_GA + e)

            def q_split(t):
                if t == 0:
                    wait_output(act, ("ga", DT - 1))
                else:
                    wait_output(act, ("s", NH * (t - 1)))
                A.copy(qs_hi[:, t % 2], q_raw[:, :, t * P:(t + 1) * P]).then_inc(qs_hi_done, 1)

            def exponentials(u):
                n = (u // NH + 1) * P
                act.wait_ge(negmax_done, u + 1)
                A.activation(probs[:, u % 2, 0:n], probs[:, u % 2, 0:n], ACT.Exp, scale=scale,
                             bias=att_small[:, 1, u % 4:u % 4 + 1],
                             accum_out=att_small[:, 2, u % 4:u % 4 + 1]).then_inc(exp_done, 1)

            def probs_hi(u):
                n = (u // NH + 1) * P
                wait_output(act, ("pt", u))
                if u >= 2:
                    if u % 2:
                        wait_output(act, ("o", (u - 2) // 2))
                    else:
                        act.wait_ge(pv_even_done, (u - 2) // 2 + 1)
                A.copy(pt_hi[:, u % 2, 0:n], psum(("pt", u))[:, 0:n]).then_inc(pt_hi_done, 1)

            def outputs_hi(w):
                t, p = divmod(w, NH // 2)
                wait_output(act, ("o", w))
                cols = slice(t * P, (t + 1) * P)
                A.copy(at_hi[0:HD, p, cols], psum(("o", w))[0:HD, 0:P])
                A.copy(at_hi[HD:P, p, cols], psum(("o", w))[HD:P, P:2 * P]).then_inc(o_hi_done, 1)

            q_split(0)
            exponentials(0)
            for u in range(units + 2):
                if 1 <= u <= units:
                    probs_hi(u - 1)
                if u + 1 < units:
                    exponentials(u + 1)
                if u % NH == 1 and u // NH + 1 < ST:
                    q_split(u // NH + 1)
                if u >= 2 and (u - 2) % 2:
                    outputs_hi((u - 2) // 2)

            for e in range(DT):
                act.wait_ge(merged, e + 1)
                A.copy(mg_hi[:, e], stage[:, e % 2]).then_inc(mg_hi_done, 1)
                if e % 2:
                    after(C_AO + e // 2)

            def h_ready(e):
                wait_evacuated(act, ("wo", e))
                if e == 0:
                    act.wait_ge(mg_lo_done, DT)
            for d in range(DT):
                after_c = C_WO + d
                wait_output(act, ("wo", d))
                split(after_c + 2)
                h_ready(d)
                act.wait_ge(acc_done, DT + d - 1)
                A.activation(stage[:, d % 2], h[:, d], ACT.Square).then_inc(square_done, 1)
            act.wait_ge(var_done, 2)
            A.activation(small[:, 8:16], small[:, 0:8], ACT.Sqrt).then_inc(sqrt_done, 1)
            norm_split(1, xm_hi)

            def tap2(g, m, col, more=0, laps=0, wait_slot=True):
                wait_output(act, ("up", g, m), more)
                A.activation(ff_t[:, m], psum(("up", g, m))[:], ACT.Copy, scale=const[:, col]).then_inc(tap2_done, 1)

            def ffn_group(g, c, first=False, i=None):
                j = 0 if i is None else i
                lap = i
                groups = g + 2 * j
                for m in range(4):
                    if not first and m in (1, 3):
                        act.wait_ge(u_lo_done, 2 * groups - 1 + m // 2)
                    if not first and m in (0, 2):
                        act.wait_ge(silu_done, 2 * groups - 1 + m // 2)
                    col = T_FCONV + 12 * g + 3 * m + 2
                    col = slice(col, col + 1) if i is None else ds(col + 24 * i, 1)
                    tap2(g, m, col, 24 * j)
                    split(c + m + 2, lap)
                    if m in (1, 3):
                        if not first:
                            act.wait_ge(ff_done, 2 * groups - 1 + m // 2)
                        wait_evacuated(act, ("up", g, m - 1), 6 * j)
                        A.activation(stage[:, m // 2], ff_t[:, m - 1], ACT.Silu).then_inc(silu_done, 1)
                    if m == 2:
                        ffn_hi(g, 0, groups, j)

            def ffn_hi(g, a, groups, j):
                act.wait_ge(ff_done, 2 * groups + a + 1)
                A.copy(u_hi[:, g % 2, a], ff_t[:, 2 * a + 1]).then_inc(u_hi_done, 1)

            ffn_group(0, C_FF, first=True)
            ffn_hi(0, 1, 0, 0)
            with act.Fori(0, 5) as i:
                for n in range(2):
                    g = 1 + n
                    ffn_group(g, C_FF + 4 + 6 * n, i=i)
                    ffn_hi(g, 1, g + 2 * i, i)
                    for k in range(2):
                        wait_output(act, ("dn", n, 4 * k + 3), 24 * i)
                        c = C_FF + 8 + 6 * n + k
                        split(c + 2, i)
            for d in range(DT):
                wait_evacuated(act, ("dn", FT // 2 - 1, d))
                act.wait_ge(acc_done, 2 * DT + d - 1)
                A.activation(stage[:, d % 2], h[:, d], ACT.Square).then_inc(square_done, 1)
            act.wait_ge(var_done, 3)
            A.activation(small[:, 8:16], small[:, 0:8], ACT.Sqrt).then_inc(sqrt_done, 1)

        @block.gpsimd
        def _(pool):
            G_ = nc.gpsimd

            def lo(c, lap=None):
                pool.wait_ge(w_hi_done, c + 1 + (0 if lap is None else 12 * lap))
                G_.tensor_tensor(w_lo[:, c % 2], w_raw[:, c % 3], w_hi[:, c % 2].bitcast(f32),
                                 ALU.subtract).then_inc(w_lo_done, 1)

            G_.memset(ident[:], 0.0).then_inc(ident_zero, 1)
            G_.memset(ones[:], 1.0).then_inc(fixed_ready, 1)
            G_.memset(mask[:, 0:mask_at(2)], 0.0).then_inc(ident_zero, 1)
            pool.wait_ge(ident_zero, 2)
            G_.affine_select(out=ident[:], in_=ident[:], compare_op=ALU.not_equal, fill=1.0, base=0,
                             pattern=[[-1, P]], channel_multiplier=1).then_inc(fixed_ready, 1)
            for t in range(2):
                diag = mask[:, mask_at(t) + t * P:mask_at(t + 1)]
                last = G_.affine_select(out=diag, in_=diag, compare_op=ALU.is_ge, fill=MASKED, base=0,
                                        pattern=[[-1, P]], channel_multiplier=1)
            last.then_inc(fixed_ready, 1)
            for c in range(C_CONV + 2):
                lo(c)
            for t in range(2, ST):
                pool.wait_ge(score_step, NH * (t - 1))
                diag = mask[:, mask_at(t) + t * P:mask_at(t + 1)]
                G_.affine_select(out=diag, in_=diag, compare_op=ALU.is_ge, fill=ACAUSAL, base=0,
                                 pattern=[[-1, P]], channel_multiplier=1).then_inc(causal_done, 1)
            for c in range(C_CONV + 2, C_GROUP + 4):
                lo(c)
                if c == C_GROUP + 3:
                    for p in range(CT):
                        pool.wait_ge(conv_hi_done, p + 1)
                        G_.tensor_tensor(cv_lo[:, p], conv_b[:, p], cv_hi[:, p].bitcast(f32),
                                         ALU.subtract).then_inc(conv_lo_done, 1)
            for j in range(4):
                lo(C_GROUP + 3 * j + 4)
                for n in range(2):
                    e = 2 * j + n
                    wait_evacuated(pool, ("gc", e))
                    wait_evacuated(pool, ("co", e))
                    G_.tensor_tensor(conv_c[:, 2 + n], conv_c[:, 2 + n], conv_c[:, n],
                                     ALU.mult).then_inc(bc_done, 1)
                if j < 3:
                    lo(C_GROUP + 3 * j + 5)
                    lo(C_GROUP + 3 * j + 6)
            for c in range(C_GROUP + 14, C_K + 2):
                lo(c)
            for p in range(PT_):
                lo(C_K + p + 2)
                pool.wait_ge(k_staged, p + 1)
                wait_evacuated(pool, ("k", p))
                G_.tensor_tensor(k_lo[:, p], stage[:, p % 2], k_hi[:, p].bitcast(f32),
                                 ALU.subtract).then_inc(k_lo_done, 1)

            def v_lo_part(p):
                pool.wait_ge(v_staged, p + 1)
                wait_evacuated(pool, ("vt", p))
                G_.tensor_tensor(v_lo[:, :, p * P:(p + 1) * P],
                                 stage[:, 1].rearrange("p (t c) -> p t c", c=P),
                                 v_hi[:, :, p * P:(p + 1) * P].bitcast(f32), ALU.subtract).then_inc(v_lo_done, 1)

            for p in range(PT_):
                lo(C_V + p + 2)
                if p:
                    v_lo_part(p - 1)
            lo(C_GA + 2)
            v_lo_part(PT_ - 1)
            for c in range(C_GA + 3, C_FF + 6):
                lo(c)

            def u_lo_part(g, a, n):
                pool.wait_ge(u_hi_done, n)
                G_.tensor_tensor(u_lo[:, g % 2, a], ff_t[:, 2 * a + 1], u_hi[:, g % 2, a].bitcast(f32),
                                 ALU.subtract).then_inc(u_lo_done, 1)

            u_lo_part(0, 0, 1)
            u_lo_part(0, 1, 2)
            with pool.Fori(0, 5) as i:
                for n in range(2):
                    g = 1 + n
                    for m in range(6):
                        lo(C_FF + 6 + 6 * n + m, i)
                        if m == 2:
                            u_lo_part(g, 0, 4 * i + 2 * g + 1)
                        if m == 3:
                            u_lo_part(g, 1, 4 * i + 2 * g + 2)

        @block.vector
        def _(dve):
            V = nc.vector

            steps = {}

            def step(s, ins):
                steps[s.name] = steps.get(s.name, 0) + 1
                ins.then_inc(s, 1)
                dve.wait_ge(s, steps[s.name])

            def accumulate(n, d):
                dve.wait_ge(square_done, DT * n + d + 1)
                if DT * n + d:
                    dve.wait_ge(acc_done, DT * n + d)
                if d == 0:
                    if n:
                        wait_output(dve, f"n{n - 1}_sum")
                    V.tensor_copy(nrm_acc[:], stage[:, 0]).then_inc(acc_done, 1)
                else:
                    V.tensor_tensor(nrm_acc[:], nrm_acc[:], stage[:, d % 2], ALU.add).then_inc(acc_done, 1)

            def norm_rms(n):
                v, s, y, t = small[:, 0:8], small[:, 8:16], small[:, 16:24], small[:, 24:32]
                a = f"n{n}_sum"
                wait_output(dve, a)
                if n:
                    dve.wait_ge(diag_done, n)
                V.tensor_scalar(v, psum(a)[:, 0:ST], 1.0 / D, EPS, ALU.mult, ALU.add).then_inc(freed(a), 1)
                wait_evacuated(dve, a)
                V.tensor_copy(t, v).then_inc(var_done, 1)
                dve.wait_ge(sqrt_done, n + 1)
                step(newton, V.reciprocal(y, s))
                step(newton, V.tensor_tensor(t, y, y, ALU.mult))
                step(newton, V.tensor_tensor(t, t, v, ALU.mult))
                step(newton, V.tensor_scalar(t, t, -0.5, 1.5, ALU.mult, ALU.add))
                step(newton, V.tensor_tensor(y, y, t, ALU.mult))
                if n == 0:
                    dve.wait_ge(fixed_ready, 3)
                else:
                    wait_output(dve, f"n{n - 1}_bc")
                for t in range(ST):
                    last = V.tensor_scalar(nrm_diag[:, t], ident[:], y[:, t:t + 1], None, ALU.mult)
                last.then_inc(diag_done, 1)

            def norm_scale(n, src, g0, hi, lo_):
                b = f"n{n}_bc"
                wait_output(dve, b)

                def low(d):
                    dve.wait_ge(norm_hi, DT * n + d + 1)
                    V.tensor_tensor(lo_[:, d], nrm_x[:, d % 2], hi[:, d].bitcast(f32),
                                    ALU.subtract).then_inc(norm_lo, 1)

                for d in range(DT):
                    if DT * n + d >= 2:
                        dve.wait_ge(norm_lo, DT * n + d - 1)
                    V.scalar_tensor_tensor(nrm_x[:, d % 2], src[:, d], const[:, g0 + d:g0 + d + 1],
                                           psum(b)[:], ALU.mult, ALU.mult).then_inc(scaled_done, 1)
                    if d:
                        low(d - 1)
                low(DT - 1)
                if n:
                    wait_evacuated(dve, f"n{n - 1}_bc")
                V.tensor_copy(small[:, 32:33], psum(b)[:, 0:1]).then_inc(freed(b), 1)

            dve.wait_ge(const_in, 16)
            for d in range(DT):
                accumulate(0, d)
            norm_rms(0)
            norm_scale(0, x_in, T_GMIX, xn_hi, xn_lo)
            dve.wait_ge(ik_hi_done, 1)
            wait_output(dve, "ikw")
            dve.wait_ge(iw_copied, 1)
            V.tensor_tensor(ik_lo[0:HD], psum("ikw")[0:HD], ik_hi[0:HD].bitcast(f32),
                            ALU.subtract).then_inc(freed("ikw"), 1)
            for p in range(PT_):
                dve.wait_ge(iq_hi_done, p + 1)
                V.tensor_tensor(iq_lo[:, p], psum(("iq", p))[:], iq_hi[:, p].bitcast(f32),
                                ALU.subtract).then_inc(freed(("iq", p)), 1)
            wait_output(dve, "iw_tok")
            V.tensor_copy(iw_tok[:].rearrange("p t h -> p (t h)"), psum("iw_tok")[:, 0:ST * NH]).then_inc(freed("iw_tok"), 1)
            wait_evacuated(dve, "iw_tok")
            n_dots = 0
            for t in range(2, ST):
                score = mask[:, mask_at(t):mask_at(t + 1)]
                n = (t + 1) * P
                for hh in range(NH):
                    wait_evacuated(dve, ("dots", t, hh))
                    r = rel[:, n_dots % 2, 0:n]
                    w = iw_tok[:, t, hh:hh + 1]
                    if hh == 0:
                        step(score_step, V.tensor_scalar(score, r, w, None, ALU.mult))
                    else:
                        step(score_step, V.scalar_tensor_tensor(score, r, w, score, ALU.mult, ALU.add))
                    n_dots += 1

            done_rounds = [0]

            def topk_rounds(t, rounds):
                score = mask[:, mask_at(t):mask_at(t + 1)]
                first = 2 * done_rounds[0]
                if first == 0:
                    dve.wait_ge(causal_done, ST - 2)
                for r in range(rounds):
                    if first or r:
                        dve.wait_ge(topk_step, first + 2 * r)
                    V.max(top8[:], score).then_inc(topk_step, 1)
                    dve.wait_ge(topk_step, first + 2 * r + 1)
                    V.match_replace(score, top8[:], score, TAKEN).then_inc(topk_step, 1)
                done_rounds[0] += rounds
                dve.wait_ge(topk_step, 2 * done_rounds[0])

            def choose(t):
                score = mask[:, mask_at(t):mask_at(t + 1)]
                V.tensor_scalar(score, score, UNCHOSEN, MASKED, ALU.is_gt, ALU.mult).then_inc(mask_done, 1)

            def convolve(p):
                for n in range(3):
                    wait_evacuated(dve, ("conv", 3 * p + n))

                def tap(k):
                    return const[:, T_CONV + k * CT + p:T_CONV + k * CT + p + 1]

                u, y, b = conv_c[:, p], conv_h[:, p], conv_b[:, p]
                step(conv_step, V.tensor_tensor(u, u, y, ALU.mult))
                step(conv_step, V.tensor_scalar(y, u, tap(2), None, ALU.mult))
                step(conv_step, V.scalar_tensor_tensor(y[:, 1:S], u[:, 0:S - 1], tap(1), y[:, 1:S], ALU.mult, ALU.add))
                step(conv_step, V.scalar_tensor_tensor(y[:, 2:S], u[:, 0:S - 2], tap(0), y[:, 2:S], ALU.mult, ALU.add))
                step(conv_step, V.tensor_tensor(b, b, y, ALU.mult))

            ROUNDS = TOPK // 8
            topk_rounds(2, ROUNDS)
            choose(2)
            convolve(0)
            topk_rounds(3, ROUNDS)
            choose(3)
            convolve(1)
            topk_rounds(4, ROUNDS // 2)
            convolve(2)
            topk_rounds(4, ROUNDS // 2)
            convolve(3)
            choose(4)
            for t in range(5, ST):
                topk_rounds(t, ROUNDS)
                choose(t)
            dve.wait_ge(mask_done, ST - 2)

            def q_split(t):
                dve.wait_ge(qs_hi_done, t + 1)
                V.tensor_tensor(qs_lo[:, t % 2], q_raw[:, :, t * P:(t + 1) * P], qs_hi[:, t % 2].bitcast(f32),
                                ALU.subtract).then_inc(qs_lo_done, 1)

            def masked_max(u):
                t = u // NH
                n = (t + 1) * P
                wait_output(dve, ("s", u))
                if u >= 2:
                    wait_output(dve, ("pt", u - 2))
                mx, nm = att_small[:, 0, u % 4:u % 4 + 1], att_small[:, 1, u % 4:u % 4 + 1]
                V.tensor_tensor_reduce(out=probs[:, u % 2, 0:n], in0=psum(("s", u))[:, 0:n],
                                       in1=mask[:, mask_at(t):mask_at(t + 1)], scale=1.0, scalar=-3e38,
                                       op0=ALU.add, op1=ALU.max, accum_out=mx).then_inc(freed(("s", u)), 1)
                wait_evacuated(dve, ("s", u))
                V.tensor_scalar(nm, mx, -scale, None, ALU.mult).then_inc(negmax_done, 1)

            def normalise(u):
                n = (u // NH + 1) * P
                dve.wait_ge(exp_done, u + 1)
                rc = att_small[:, 3, u % 4:u % 4 + 1]
                step(recip_done, V.reciprocal(rc, att_small[:, 2, u % 4:u % 4 + 1]))
                V.tensor_scalar(probs[:, u % 2, 0:n], probs[:, u % 2, 0:n], rc, None,
                                ALU.mult).then_inc(probs_done, 1)

            def probs_lo(u):
                n = (u // NH + 1) * P
                dve.wait_ge(pt_hi_done, u + 1)
                V.tensor_tensor(pt_lo[:, u % 2, 0:n], psum(("pt", u))[:, 0:n], pt_hi[:, u % 2, 0:n].bitcast(f32),
                                ALU.subtract).then_inc(freed(("pt", u)), 1)

            def outputs_lo(w):
                t, p = divmod(w, NH // 2)
                dve.wait_ge(o_hi_done, w + 1)
                cols = slice(t * P, (t + 1) * P)
                V.tensor_tensor(at_lo[0:HD, p, cols], psum(("o", w))[0:HD, 0:P],
                                at_hi[0:HD, p, cols].bitcast(f32), ALU.subtract)
                V.tensor_tensor(at_lo[HD:P, p, cols], psum(("o", w))[HD:P, P:2 * P],
                                at_hi[HD:P, p, cols].bitcast(f32), ALU.subtract).then_inc(freed(("o", w)), 1)

            q_split(0)
            masked_max(0)
            for u in range(units + 2):
                if u < units:
                    normalise(u)
                if 1 <= u <= units:
                    probs_lo(u - 1)
                if u + 1 < units:
                    masked_max(u + 1)
                if u % NH == 1 and u // NH + 1 < ST:
                    q_split(u // NH + 1)
                if u >= 2 and (u - 2) % 2:
                    outputs_lo((u - 2) // 2)

            def merge_lo(e):
                dve.wait_ge(mg_hi_done, e + 1)
                V.tensor_tensor(mg_lo[:, e], stage[:, e % 2], mg_hi[:, e].bitcast(f32),
                                ALU.subtract).then_inc(mg_lo_done, 1)

            for e in range(DT):
                wait_output(dve, ("ao", e))
                if e >= 2:
                    dve.wait_ge(mg_lo_done, e - 1)
                dve.wait_ge(gate_loaded[e % 2], 32 * (e // 2 + 1))
                V.tensor_tensor(stage[:, e % 2], psum(("ao", e))[:], gate_in[:, e % 2, 0],
                                ALU.mult).then_inc(freed(("ao", e)), 1)
                wait_evacuated(dve, ("ao", e))
                V.tensor_tensor(stage[:, e % 2], stage[:, e % 2], gate_in[:, e % 2, 1], ALU.add).then_inc(merged, 1)
                if e:
                    merge_lo(e - 1)
            merge_lo(DT - 1)

            def add_to_h(name, e, more=0):
                wait_output(dve, name, more)
                V.tensor_tensor(h[:, e], psum(name)[:], h[:, e], ALU.add).then_inc(freed(name), 1)

            for e in range(DT):
                dve.wait_ge(x_loaded[e], 32)
                add_to_h(("wo", e), e)
                if e:
                    accumulate(1, e - 1)
            accumulate(1, DT - 1)
            norm_rms(1)
            norm_scale(1, h, T_GFFN, xm_hi, xm_lo)

            def conv_taps(g, m, groups, i=None):
                j = 0 if i is None else i
                base_col = T_FCONV + 12 * g + 3 * m

                def tap(k):
                    return const[:, base_col + k:base_col + k + 1] if i is None else const[:, ds(base_col + k + 24 * i, 1)]

                t, src = ff_t[:, m], psum(("up", g, m))
                dve.wait_ge(tap2_done, 4 * groups + m + 1)
                V.scalar_tensor_tensor(t[:, 1:S], src[:, 0:S - 1], tap(1), t[:, 1:S], ALU.mult,
                                       ALU.add).then_inc(tap1_done, 1)
                dve.wait_ge(tap1_done, 4 * groups + m + 1)
                V.scalar_tensor_tensor(t[:, 2:S], src[:, 0:S - 2], tap(0), t[:, 2:S], ALU.mult,
                                       ALU.add).then_inc(freed(("up", g, m)), 1)

            def gate_times_value(g, a, groups, i=None):
                j = 0 if i is None else i
                dve.wait_ge(silu_done, 2 * groups + a + 1)
                wait_evacuated(dve, ("up", g, 2 * a + 1), 6 * j)
                V.tensor_tensor(ff_t[:, 2 * a + 1], ff_t[:, 2 * a + 1], stage[:, a], ALU.mult).then_inc(ff_done, 1)

            def ffn_group(g, i=None):
                groups = g if i is None else g + 2 * i
                conv_taps(g, 0, groups, i)
                conv_taps(g, 1, groups, i)
                gate_times_value(g, 0, groups, i)
                conv_taps(g, 2, groups, i)
                conv_taps(g, 3, groups, i)
                gate_times_value(g, 1, groups, i)

            ffn_group(0)
            with dve.Fori(0, 5) as i:
                for n in range(2):
                    ffn_group(1 + n, i)
                    for e in range(DT):
                        add_to_h(("dn", n, e), e, 24 * i)
            for e in range(DT):
                add_to_h(("dn", FT // 2 - 1, e), e)
                if e:
                    accumulate(2, e - 1)
            accumulate(2, DT - 1)
            norm_rms(2)
            wait_output(dve, "n2_bc")
            for d in range(DT):
                if d >= 2:
                    dve.wait_ge(out_stored[d % 2], 16 * (d // 2))
                elif d == 0:
                    dve.wait_ge(norm_lo, 2 * DT)
                V.scalar_tensor_tensor(nrm_x[:, d % 2], h[:, d], const[:, T_GFIN + d:T_GFIN + d + 1],
                                       psum("n2_bc")[:], ALU.mult, ALU.mult).then_inc(out_scaled, 1)


def pack(w_in, w_attn_out, w_conv_out, w_o, w_up, w_down):
    def cols(w, c0):
        return w[:, c0:c0 + P].reshape(-1, P, P).transpose(1, 0, 2)

    ikw = np.zeros((D, P), w_in.dtype)
    ikw[:, 0:HD] = w_in[:, IK0:IK0 + HD]
    ikw[:, HD:HD + NH] = w_in[:, IW0:IW0 + NH]
    out = [cols(ikw, 0)]
    out += [cols(w_in, IQ0 + p * P) for p in range(PT_)]
    for p in range(CT):
        out += [cols(w_in, c + p * P) for c in (CH0, CC0, CB0)]

    def two(w, j):
        return np.concatenate([cols(w, (2 * j) * P), cols(w, (2 * j + 1) * P)], axis=1)

    for j in range(4):
        out += [cols(w_in, G0 + D + (2 * j + n) * P) for n in range(2)] + [two(w_conv_out, j)]
    for c in (Q0, K0, V0):
        out += [cols(w_in, c + p * P) for p in range(PT_)]
    out += [cols(w_in, G0 + e * P) for e in range(DT)]
    out += [two(w_attn_out, j) for j in range(4)]
    out += [cols(w_o, e * P) for e in range(DT)]

    def up(g):
        return [cols(w_up, c) for a in range(2) for c in ((2 * g + a) * P, FF + (2 * g + a) * P)]

    def down(g):
        rows = w_down[2 * g * P:(2 * g + 2) * P]
        return [np.concatenate([cols(rows, (4 * n + e) * P) for e in range(4)], axis=1) for n in range(2)]

    out += up(0)
    for g in range(1, FT // 2):
        out += up(g) + down(g - 1)
    out += down(FT // 2 - 1)
    return np.ascontiguousarray(np.stack(out).reshape(N_CHUNKS, P, 8 * P))


def kernel(**inputs):
    import concourse.bacc as bacc
    from concourse.bass_utils import run_bass_kernel_spmd

    a = {k: np.asarray(v) for k, v in inputs.items()}
    x = a["x"]
    xT = np.ascontiguousarray(x[0].T.reshape(DT, P, S))
    wts = pack(a["w_in"][0], a["w_attn_out"][0], a["w_conv_out"][0], a["w_o"][0], a["w_up"][0], a["w_down"][0])

    def per_channel(v):
        return v.reshape(-1, P).T

    fconv = a["ffn_conv_w"][0].reshape(3, 2, FT // 2, 2, P)
    consts = np.ascontiguousarray(np.concatenate([
        per_channel(a["norm_mix_g"][0]), per_channel(a["norm_ffn_g"][0]), per_channel(a["norm_final_g"]),
        per_channel(a["b_gate"][0]), per_channel(a["conv_w"][0].reshape(-1)),
        fconv.transpose(4, 2, 3, 1, 0).reshape(P, -1)], axis=1))
    arrays = {"xT_dram": xT, "wts_dram": wts, "consts_dram": consts}

    nc = bacc.Bacc("TRN2", target_bir_lowering=False, num_devices=1)
    f32 = mybir.dt.float32
    ins = [nc.dram_tensor(n, v.shape, f32, kind="ExternalInput").ap() for n, v in arrays.items()]
    out = nc.dram_tensor("outT_dram", (DT, P, S), f32, kind="ExternalOutput").ap()
    bc_dram = nc.dram_tensor("bc_dram", (DT, P, S), f32, kind="Internal").ap()
    ga_dram = nc.dram_tensor("ga_dram", (DT, P, S), f32, kind="Internal").ap()
    build(nc, *ins, out, bc_dram, ga_dram)
    r = run_bass_kernel_spmd(nc, [arrays], core_ids=[0])
    got = np.asarray(r.results[0]["outT_dram"])
    return np.ascontiguousarray(got.reshape(D, S).T).reshape(x.shape)
```

```python
from contextlib import ExitStack, contextmanager

import numpy as np

import concourse.bass as bass
from concourse import mybir

P = 128
D = 1024
S = 1024
DT = D // P
ST = S // P
NH = 8
HD = 64
PT_ = NH * HD // P
CW = 512
CT = CW // P
FF = 2816
FT = FF // P
TOPK = 256
EPS = 1e-6
HALF = 512

Q0, K0, V0 = 0, 512, 1024
IQ0, IK0, IW0 = 1536, 2048, 2112
CH0, CB0, CC0, G0 = 2120, 2632, 3144, 3656

PAIRS = ST * PT_

C_IKW = 0
C_IQ = 1
C_CONV = 5
C_GROUP = 17
C_Q = 29
C_K = 33
C_V = 37
C_GA = 41
C_AO = 49
C_WO = 53
C_FF = 61
N_CHUNKS = 127

T_GMIX, T_GFFN, T_GFIN, T_BIAS = 0, 8, 16, 24
T_CONV = 40
T_FCONV = T_CONV + 3 * CT
N_CONST = T_FCONV + 3 * 2 * FT

TAKEN = -3e38
ACAUSAL = -1e38
UNCHOSEN = -2e38
MASKED = -1e30


def mask_at(t):
    return P * t * (t + 1) // 2


def wide(w):
    return w // PT_ >= 4


def s_names(w):
    return [("s", w, 0), ("s", w, 1)] if wide(w) else [("s", w)]


def pt_names(w):
    return [("pt", w, 0), ("pt", w, 1)] if wide(w) else [("pt", w)]


def tickets():
    order = ["n0_sum", "n0_bc", "ikw", *[("iq", p) for p in range(PT_)], "iw_tok"]
    order += [("dots", t, h) for t in range(2, ST) for h in range(NH)]
    order += [("conv", n) for n in range(3 * CT)]
    for j in range(4):
        order += [("gc", 2 * j), ("gc", 2 * j + 1), ("co", 2 * j), ("co", 2 * j + 1)]
    order += [("q", p) for p in range(PT_)] + [("k", p) for p in range(PT_)]
    order += [("v", 0)]
    for p in range(1, PT_):
        order += [("v", p), ("vt", p - 1)]
    order += [("ga", 0), ("vt", PT_ - 1)] + [("ga", e) for e in range(1, DT)]
    order += s_names(0) + s_names(1)
    for w in range(PAIRS + 1):
        t, p = divmod(w, PT_)
        a, b = (pt_names(w) if w < PAIRS else []), (s_names(w + 2) if w + 2 < PAIRS else [])
        order += a[:1] + b[:1] + a[1:] + b[1:]
        if w >= 1:
            order += [("o", w - 1)]
        if w >= 1 and p == 0:
            order += [("sums", t - 1)]
    order += [("ao", e) for e in range(DT)] + [("wo", e) for e in range(DT)]
    order += ["n1_sum", "n1_bc"]
    order += [("up", 0, m) for m in range(4)]
    for g in range(1, FT // 2):
        order += [("up", g, m) for m in range(4)] + [("dn", g - 1, e) for e in range(DT)]
    order += [("dn", FT // 2 - 1, e) for e in range(DT)]
    order += ["n2_sum", "n2_bc"]
    return {name: n for n, name in enumerate(order)}


def build(nc, xT, wts, consts, outT, bc_dram, ga_dram):
    f32, f32r = mybir.dt.float32, mybir.dt.float32r
    ALU, ACT = mybir.AluOpType, mybir.ActivationFunctionType
    ds = bass.ds
    U = tickets()
    scale = float(HD) ** -0.5
    iw_scale = float(NH) ** -0.5 * float(HD) ** -0.5

    KB = 1024
    base = 16512
    X = base
    Q = X + 64 * KB
    M = Q + 80 * KB
    W = M + 18 * KB
    G = W + 28 * KB
    Z = G + 8 * KB

    def at(name, shape, dt, where):
        return nc.alloc_sbuf_tensor_at(name, [P, *shape], dt, offset=where)

    w_raw = at("w_raw", [3, 8, P], f32, W)
    w_hi = at("w_hi", [2, 8, P], f32r, W + 12 * KB)
    w_lo = at("w_lo", [2, 8, P], f32r, W + 20 * KB)
    stage = at("stage", [2, S], f32, G)
    const = at("const", [N_CONST], f32, Z)
    ident = at("ident", [P], f32, Z + 1024)
    ones = at("ones", [P], f32, Z + 1536)
    small = at("small", [64], f32, Z + 2048)
    iw_tok = at("iw_tok", [ST, NH], f32, Z + 2304)
    negmax = at("negmax", [4], f32, Z + 2560)
    sums = at("sums", [2, NH], f32, Z + 2592)
    top8 = at("top8", [8], f32, Z + 2656)
    recips = at("recips", [2, NH], f32, Z + 2688)

    xn_hi = at("xn_hi", [DT, S], f32r, X)
    xn_lo = at("xn_lo", [DT, S], f32r, X + 32 * KB)
    x_in = at("x_in", [DT, S], f32, Q)
    nrm_acc = at("nrm_acc", [S], f32, Q + 64 * KB)
    nrm_diag = at("nrm_diag", [ST, P], f32, Q + 68 * KB)
    nrm_x = at("nrm_x", [2, S], f32, Q + 72 * KB)
    iq_hi = at("iq_hi", [PT_, S], f32r, Q)
    iq_lo = at("iq_lo", [PT_, S], f32r, Q + 16 * KB)
    ik_hi = at("ik_hi", [S], f32r, Q + 32 * KB)
    ik_lo = at("ik_lo", [S], f32r, Q + 36 * KB)
    rel = at("rel", [2, S], f32, Q + 40 * KB)
    conv_h = at("conv_h", [CT, S], f32, Q)
    conv_c = at("conv_c", [CT, S], f32, Q + 16 * KB)
    conv_b = at("conv_b", [CT, S], f32, Q + 32 * KB)
    cv_hi = at("cv_hi", [CT, S], f32r, Q + 48 * KB)
    cv_lo = at("cv_lo", [CT, S], f32r, Q + 64 * KB)
    q_raw = at("q_raw", [PT_, S], f32, Q)
    k_hi = at("k_hi", [PT_, S], f32r, Q + 16 * KB)
    k_lo = at("k_lo", [PT_, S], f32r, Q + 32 * KB)
    v_hi = at("v_hi", [ST, NH * HD], f32r, Q + 48 * KB)
    v_lo = at("v_lo", [ST, NH * HD], f32r, Q + 64 * KB)
    mask = at("mask", [ST * (ST + 1) // 2 * P], f32, M)
    probs = at("probs", [2, 2, S], f32, X)
    qs_hi = at("qs_hi", [2, PT_, P], f32r, X + 16 * KB)
    qs_lo = at("qs_lo", [2, PT_, P], f32r, X + 20 * KB)
    rc_wide = at("rc_wide", [2, PT_, P], f32, X + 24 * KB)
    rc_tok = at("rc_tok", [2, PT_, P], f32, X + 28 * KB)
    pt_hi = at("pt_hi", [2, ST, 2, P], f32r, X + 32 * KB)
    pt_lo = at("pt_lo", [2, ST, 2, P], f32r, X + 48 * KB)
    at_hi = at("at_hi", [PT_, S], f32r, X + 32 * KB)
    at_lo = at("at_lo", [PT_, S], f32r, X + 48 * KB)
    gate_in = at("gate_in", [2, 2, S], f32, M)
    mg_hi = at("mg_hi", [DT, S], f32r, Q)
    mg_lo = at("mg_lo", [DT, S], f32r, Q + 32 * KB)
    h = at("h", [DT, S], f32, X)
    xm_hi = at("xm_hi", [DT, S], f32r, Q)
    xm_lo = at("xm_lo", [DT, S], f32r, Q + 32 * KB)
    ff_t = at("ff_t", [4, S], f32, M)
    u_hi = at("u_hi", [2, 2, S], f32r, X + 32 * KB)
    u_lo = at("u_lo", [2, 2, S], f32r, X + 48 * KB)

    ctx = ExitStack()
    with ctx:
        pair = [ctx.enter_context(nc.psum_tensor(f"pair{i}", [P, S], f32)) for i in range(4)]

        def sem(name):
            return ctx.enter_context(nc.semaphore(name))

        const_in = sem("const_in")
        x_loaded = [sem(f"x_loaded{d}") for d in range(DT)]
        w_loaded = [sem(f"w_loaded{s}") for s in range(3)]
        w_hi_done, w_lo_done = sem("w_hi_done"), sem("w_lo_done")
        out_ready = sem("out_ready")
        evacuated = [sem(f"evacuated{i}") for i in range(4)]
        fixed_ready, ident_zero = sem("fixed_ready"), sem("ident_zero")
        square_done, acc_done, newton = sem("square_done"), sem("acc_done"), sem("newton")
        var_done, sqrt_done, diag_done = sem("var_done"), sem("sqrt_done"), sem("diag_done")
        scaled_done, norm_hi, norm_lo = sem("scaled_done"), sem("norm_hi"), sem("norm_lo")
        ik_hi_done, iw_copied = sem("ik_hi_done"), sem("iw_copied")
        ik_copied = [sem("ik_hi_copied"), sem("ik_lo_copied")]
        iq_hi_done = sem("iq_hi_done")
        score_step, causal_done = sem("score_step"), sem("causal_done")
        topk_step, mask_done = sem("topk_step"), sem("mask_done")
        conv_step, conv_hi_done, conv_lo_done = sem("conv_step"), sem("conv_hi_done"), sem("conv_lo_done")
        gc_done, co_copied, bc_done = sem("gc_done"), sem("co_copied"), sem("bc_done")
        bc_stored = [sem("bc_stored0"), sem("bc_stored1")]
        ga_stored = [sem("ga_stored0"), sem("ga_stored1")]
        k_staged, k_lo_done, v_staged, v_lo_done = sem("k_staged"), sem("k_lo_done"), sem("v_staged"), sem("v_lo_done")
        qs_hi_done, qs_lo_done = sem("qs_hi_done"), sem("qs_lo_done")
        first_max_done = sem("first_max_done")
        exp_done, recip_done = sem("exp_done"), sem("recip_done")
        rc_widened, at_scaled = sem("rc_widened"), sem("at_scaled")
        pt_hi_done, at_hi_done, at_lo_done = sem("pt_hi_done"), sem("at_hi_done"), sem("at_lo_done")
        gate_loaded = [sem("gate_loaded0"), sem("gate_loaded1")]
        merged, mg_hi_done, mg_lo_done = sem("merged"), sem("mg_hi_done"), sem("mg_lo_done")
        tap2_done, tap1_done = sem("tap2_done"), sem("tap1_done")
        silu_done, ff_done, u_hi_done, u_lo_done = sem("silu_done"), sem("ff_done"), sem("u_hi_done"), sem("u_lo_done")
        out_scaled = sem("out_scaled")
        out_stored = [sem("out_stored0"), sem("out_stored1")]

        block = ctx.enter_context(nc.Block())

        def wait_output(eng, name, more=0):
            eng.wait_ge(out_ready, U[name] + 1 + more)

        def wait_evacuated(eng, name, laps=0):
            eng.wait_ge(evacuated[U[name] % 4], U[name] // 4 + 1 + laps)

        def psum(name):
            return pair[U[name] % 4]

        def freed(name):
            return evacuated[U[name] % 4]

        def logits_of(w, a):
            n = (w // PT_ + 1) * P
            return (("s", w, a), slice(0, n)) if wide(w) else (("s", w), slice(a * HALF, a * HALF + n))

        def transposed(name):
            w = name[1]
            nk = w // PT_ + 1
            if wide(w):
                return w, psum(name)[:, 0:nk * P].rearrange("p (k q) -> p k q", q=P), \
                    lambda buf: buf[:, w % 2, 0:nk, name[2]]
            both = psum(name)[:].rearrange("p (a k q) -> p a k q", a=2, q=P)
            return w, both[:, :, 0:nk], lambda buf: buf[:, w % 2, 0:nk].rearrange("p k a q -> p a k q")

        pt_number = {name: n + 1 for n, name in enumerate(x for w in range(PAIRS) for x in pt_names(w))}

        last_of = [("ikw")] + [("iq", p) for p in range(PT_)] + [("conv", n) for n in range(12)]
        for j in range(4):
            last_of += [("gc", 2 * j), ("gc", 2 * j + 1), ("co", 2 * j + 1)]
        last_of += [("q", p) for p in range(4)] + [("k", p) for p in range(4)] + [("v", p) for p in range(4)]
        last_of += [("ga", e) for e in range(8)] + [("ao", 2 * j + 1) for j in range(4)] + [("wo", e) for e in range(8)]
        last_of += [("up", 0, m) for m in range(4)]
        for g in range(1, FT // 2):
            last_of += [("up", g, m) for m in range(4)] + [("dn", g - 1, 3), ("dn", g - 1, 7)]
        last_of += [("dn", FT // 2 - 1, 3), ("dn", FT // 2 - 1, 7)]
        assert len(last_of) == N_CHUNKS

        @block.sync
        def _(sp):
            def load_chunk(c, lap=None):
                if c >= 3:
                    sp.wait_ge(w_lo_done, c - 2 + (0 if lap is None else 12 * lap))
                src = wts[c] if lap is None else wts[ds(c + 12 * lap, 1)].rearrange("a p n -> p (a n)")
                sp.dma_start(w_raw[:, c % 3].rearrange("p a b -> p (a b)"), src).then_inc(w_loaded[c % 3], 16)

            sp.dma_start(const[:], consts).then_inc(const_in, 16)
            for d in range(DT):
                sp.dma_start(x_in[:, d], xT[d]).then_inc(x_loaded[d], 16)
            for c in range(C_AO + 5):
                load_chunk(c)
                j, at_end = divmod(c - (C_GROUP + 2 + 5), 3)
                if at_end == 0 and 0 <= j < 4:
                    for e in (2 * j, 2 * j + 1):
                        sp.wait_ge(bc_done, e + 1)
                        sp.dma_start(bc_dram[e], conv_c[:, 2 + e % 2]).then_inc(bc_stored[e % 2], 16)
                e = c - (C_GA + 5)
                if 0 <= e < DT:
                    wait_evacuated(sp, ("ga", e))
                    sp.dma_start(ga_dram[e], stage[:, e % 2]).then_inc(ga_stored[e % 2], 16)
            wait_evacuated(sp, s_names(PAIRS - 1)[-1])
            for n in range(2):
                sp.wait_ge(bc_stored[n], 16 * DT // 2)
                sp.wait_ge(ga_stored[n], 16 * DT // 2)
            for e in range(DT):
                if e >= 2:
                    sp.wait_ge(merged, e - 1)
                sp.dma_start(gate_in[:, e % 2, 0], ga_dram[e]).then_inc(gate_loaded[e % 2], 16)
                sp.dma_start(gate_in[:, e % 2, 1], bc_dram[e]).then_inc(gate_loaded[e % 2], 16)
                if e == 1:
                    sp.wait_ge(at_scaled, ST)
                    for d in range(DT):
                        sp.dma_start(h[:, d], xT[d]).then_inc(x_loaded[d], 16)
            for c in range(C_AO + 5, C_FF + 6):
                load_chunk(c)
            with sp.Fori(0, 5) as i:
                for n in range(12):
                    load_chunk(C_FF + 6 + n, i)
            for d in range(DT):
                sp.wait_ge(out_scaled, d + 1)
                sp.dma_start(outT[d], nrm_x[:, d % 2]).then_inc(out_stored[d % 2], 16)
            for n in range(2):
                sp.wait_ge(out_stored[n], 16 * DT // 2)

        @block.tensor
        def _(pe):
            def take_pair(name, more=0, laps=0):
                if U[name] >= 4:
                    pe.wait_ge(evacuated[U[name] % 4], U[name] // 4 + laps)

            def three(out, w_h, w_l, x_h, x_l, first, last):
                nc.tensor.matmul(out, w_h, x_h, start=first, stop=False)
                nc.tensor.matmul(out, w_h, x_l, start=False, stop=False)
                return nc.tensor.matmul(out, w_l, x_h, start=False, stop=last)

            def product(name, slot, blocks, x_h, x_l, each_k=None):
                for half in range(2):
                    cols = slice(half * HALF, (half + 1) * HALF)
                    for n, b in enumerate(blocks):
                        if each_k is not None and half == 0:
                            each_k(n)
                        last = three(psum(name)[:, cols], w_hi[:, slot, b], w_lo[:, slot, b],
                                     x_h(n)[:, cols], x_l(n)[:, cols], n == 0, n == len(blocks) - 1)
                last.then_inc(out_ready, 1)

            def chunk(c, names, x_h, x_l, each_k=None, lap=None, laps_psum=0):
                pe.wait_ge(w_lo_done, c + 1 + (0 if lap is None else 12 * lap))
                per = 8 // len(names)
                for n, name in enumerate(names):
                    take_pair(name, laps=laps_psum)
                    product(name, c % 2, range(n * per, (n + 1) * per), x_h, x_l, each_k)

            def norm(n):
                a, b = f"n{n}_sum", f"n{n}_bc"
                take_pair(a)
                if n == 0:
                    pe.wait_ge(fixed_ready, 3)
                pe.wait_ge(acc_done, DT * (n + 1))
                for t in range(ST):
                    last = nc.tensor.matmul(psum(a)[:, t:t + 1], nrm_acc[:, t * P:(t + 1) * P], ones[:, 0:1],
                                            start=True, stop=True)
                last.then_inc(out_ready, 1)
                take_pair(b)
                pe.wait_ge(diag_done, n + 1)
                for half in range(2):
                    last = nc.tensor.matmul(psum(b)[:, half * HALF:(half + 1) * HALF], ones[:],
                                            nrm_diag[:, 4 * half:4 * half + 4].rearrange("p a b -> p (a b)"),
                                            start=True, stop=True)
                last.then_inc(out_ready, 1)

            def from_xn():
                return (lambda k: xn_hi[:, k]), (lambda k: xn_lo[:, k])

            norm(0)
            chunk(C_IKW, ["ikw"], *from_xn(), each_k=lambda k: pe.wait_ge(norm_lo, k + 1))
            for p in range(PT_):
                chunk(C_IQ + p, [("iq", p)], *from_xn())
            take_pair("iw_tok")
            pe.wait_ge(iw_copied, 1)
            for t in range(ST):
                last = nc.tensor.transpose(psum("iw_tok")[:, t * NH:(t + 1) * NH],
                                           stage[HD:HD + NH, 0, t * P:(t + 1) * P], ident[HD:HD + NH, HD:HD + NH])
            last.then_inc(out_ready, 1)
            for s in ik_copied:
                pe.wait_ge(s, 16)
            for t in range(2, ST):
                for hh in range(NH):
                    name = ("dots", t, hh)
                    p, r = hh // 2, slice(HD * (hh % 2), HD * (hh % 2) + HD)
                    take_pair(name)
                    wait_evacuated(pe, ("iq", p))
                    for k0 in range(0, (t + 1) * P, HALF):
                        cols = slice(k0, min(k0 + HALF, (t + 1) * P))
                        q = slice(t * P, (t + 1) * P)
                        last = three(psum(name)[:, cols], iq_hi[r, p, q], iq_lo[r, p, q],
                                     ik_hi[r, cols], ik_lo[r, cols], True, True)
                    last.then_inc(out_ready, 1)
            for n in range(3 * CT):
                chunk(C_CONV + n, [("conv", n)], *from_xn())
            for j in range(4):
                chunk(C_GROUP + 3 * j, [("gc", 2 * j)], *from_xn())
                chunk(C_GROUP + 3 * j + 1, [("gc", 2 * j + 1)], *from_xn())
                chunk(C_GROUP + 3 * j + 2, [("co", 2 * j), ("co", 2 * j + 1)],
                      lambda k: cv_hi[:, k], lambda k: cv_lo[:, k],
                      each_k=(lambda k: pe.wait_ge(conv_lo_done, k + 1)) if j == 0 else None)
            for p in range(PT_):
                chunk(C_Q + p, [("q", p)], *from_xn())
            for p in range(PT_):
                chunk(C_K + p, [("k", p)], *from_xn())

            def v_transposes(p):
                take_pair(("vt", p))
                wait_evacuated(pe, ("v", p))
                for t in range(ST):
                    last = nc.tensor.transpose(psum(("vt", p))[:, t * P:(t + 1) * P],
                                               stage[:, 0, t * P:(t + 1) * P], ident[:])
                last.then_inc(out_ready, 1)

            for p in range(PT_):
                chunk(C_V + p, [("v", p)], *from_xn())
                if p:
                    v_transposes(p - 1)
            chunk(C_GA, [("ga", 0)], *from_xn())
            v_transposes(PT_ - 1)
            for e in range(1, DT):
                chunk(C_GA + e, [("ga", e)], *from_xn())

            def logits(w, a):
                t, p = divmod(w, PT_)
                r = slice(HD * a, HD * a + HD)
                name, c = logits_of(w, a)
                if a == 0:
                    pe.wait_ge(qs_lo_done, t + 1)
                if wide(w) or a == 0:
                    take_pair(name)
                for k0 in range(0, (t + 1) * P, HALF):
                    k1 = min(k0 + HALF, (t + 1) * P)
                    last = three(psum(name)[:, c.start + k0:c.start + k1],
                                 qs_hi[r, t % 2, p], qs_lo[r, t % 2, p],
                                 k_hi[r, p, k0:k1], k_lo[r, p, k0:k1], True, True)
                if wide(w) or a == 1:
                    last.then_inc(out_ready, 1)

            def transpose_probs(w, a):
                name = pt_names(w)[a if wide(w) else 0]
                c0 = 0 if wide(w) else a * HALF
                if wide(w) or a == 0:
                    take_pair(name)
                pe.wait_ge(exp_done, 2 * w + a + 1)
                for kb in range(w // PT_ + 1):
                    last = nc.tensor.transpose(psum(name)[:, c0 + kb * P:c0 + (kb + 1) * P],
                                               probs[:, w % 2, a, kb * P:(kb + 1) * P], ident[:])
                if wide(w) or a == 1:
                    last.then_inc(out_ready, 1)

            def probs_times_v(w):
                t, p = divmod(w, PT_)
                take_pair(("o", w))
                for name in pt_names(w):
                    wait_evacuated(pe, name)
                for kb in range(t + 1):
                    last = three(psum(("o", w))[:, 0:2 * P], v_hi[:, kb, p * P:(p + 1) * P],
                                 v_lo[:, kb, p * P:(p + 1) * P],
                                 pt_hi[:, w % 2, kb].rearrange("p a q -> p (a q)"),
                                 pt_lo[:, w % 2, kb].rearrange("p a q -> p (a q)"), kb == 0, kb == t)
                last.then_inc(out_ready, 1)

            def reciprocals(t):
                name = ("sums", t)
                take_pair(name)
                pe.wait_ge(rc_widened, t + 1)
                for p in range(PT_):
                    last = nc.tensor.transpose(psum(name)[:, p * P:(p + 1) * P], rc_wide[:, t % 2, p], ident[:])
                last.then_inc(out_ready, 1)

            pe.wait_ge(k_lo_done, PT_)
            pe.wait_ge(v_lo_done, PT_)
            for w in range(2):
                for a in range(2):
                    logits(w, a)
            for w in range(PAIRS + 1):
                if w < PAIRS and wide(w):
                    for a in range(2):
                        transpose_probs(w, a)
                        if w + 2 < PAIRS:
                            logits(w + 2, a)
                elif w < PAIRS:
                    for a in range(2):
                        transpose_probs(w, a)
                    for a in range(2):
                        logits(w + 2, a)
                if w >= 1:
                    probs_times_v(w - 1)
                if w >= 1 and w % PT_ == 0:
                    reciprocals(w // PT_ - 1)

            for j in range(4):
                chunk(C_AO + j, [("ao", 2 * j), ("ao", 2 * j + 1)], lambda k: at_hi[:, k], lambda k: at_lo[:, k],
                      each_k=(lambda k: pe.wait_ge(at_lo_done, k + 1)) if j == 0 else None)
            for e in range(DT):
                chunk(C_WO + e, [("wo", e)], lambda k: mg_hi[:, k], lambda k: mg_lo[:, k],
                      each_k=(lambda k: pe.wait_ge(mg_lo_done, k + 1)) if e == 0 else None)
            norm(1)

            def up(g, c, more=None, laps=0):
                for m in range(4):
                    chunk(c + m, [("up", g, m)], lambda k: xm_hi[:, k], lambda k: xm_lo[:, k],
                          each_k=(lambda k: pe.wait_ge(norm_lo, DT + k + 1)) if g == 0 and m == 0 else None,
                          lap=more, laps_psum=laps)

            def down(g, c, more=None, laps=0):
                pe.wait_ge(u_lo_done, 2 * g + 2 + (0 if more is None else 4 * more))
                for n in range(2):
                    chunk(c + n, [("dn", g, 4 * n + e) for e in range(4)],
                          lambda k: u_hi[:, g % 2, k], lambda k: u_lo[:, g % 2, k], lap=more, laps_psum=laps)

            up(0, C_FF)
            with pe.Fori(0, 5) as i:
                for n in range(2):
                    up(1 + n, C_FF + 4 + 6 * n, i, 6 * i)
                    down(n, C_FF + 8 + 6 * n, i, 6 * i)
            down(FT // 2 - 1, N_CHUNKS - 2)
            norm(2)

        @block.scalar
        def _(act):
            A = nc.scalar

            def split(c, lap=None):
                act.wait_ge(w_loaded[c % 3], 16 * (c // 3 + 1) + (0 if lap is None else 64 * lap))
                if c >= 2:
                    wait_output(act, last_of[c - 2], 0 if lap is None else 24 * lap)
                A.copy(w_hi[:, c % 2], w_raw[:, c % 3]).then_inc(w_hi_done, 1)

            def norm(n, src, arrived):
                for d in range(DT):
                    arrived(d)
                    if DT * n + d >= 2:
                        act.wait_ge(acc_done, DT * n + d - 1)
                    A.activation(stage[:, d % 2], src[:, d], ACT.Square).then_inc(square_done, 1)
                act.wait_ge(var_done, n + 1)
                A.activation(small[:, 8:16], small[:, 0:8], ACT.Sqrt).then_inc(sqrt_done, 1)

            def norm_split(n, hi):
                for d in range(DT):
                    act.wait_ge(scaled_done, DT * n + d + 1)
                    A.copy(hi[:, d], nrm_x[:, d % 2]).then_inc(norm_hi, 1)

            def after(c):
                split(c + 2)

            norm(0, x_in, lambda d: act.wait_ge(x_loaded[d], 16))
            split(0)
            split(1)
            norm_split(0, xn_hi)
            wait_output(act, "ikw")
            A.copy(ik_hi[0:HD], psum("ikw")[0:HD]).then_inc(ik_hi_done, 1)
            A.mul(stage[HD:HD + NH, 0], psum("ikw")[HD:HD + NH], iw_scale).then_inc(iw_copied, 1)
            after(C_IKW)
            act.wait_ge(ik_hi_done, 1)
            act.dma_start(ik_hi[HD:P].bitcast(f32), ik_hi[0:HD].bitcast(f32)).then_inc(ik_copied[0], 16)
            wait_evacuated(act, "ikw")
            act.dma_start(ik_lo[HD:P].bitcast(f32), ik_lo[0:HD].bitcast(f32)).then_inc(ik_copied[1], 16)
            for p in range(PT_):
                wait_output(act, ("iq", p))
                A.copy(iq_hi[:, p], psum(("iq", p))[:]).then_inc(iq_hi_done, 1)
                after(C_IQ + p)
            n_dots = 0
            for t in range(2, ST):
                for hh in range(NH):
                    name, n = ("dots", t, hh), (t + 1) * P
                    wait_output(act, name)
                    if n_dots >= 2:
                        act.wait_ge(score_step, n_dots - 1)
                    A.activation(rel[:, n_dots % 2, 0:n], psum(name)[:, 0:n], ACT.Relu).then_inc(freed(name), 1)
                    n_dots += 1
            def conv_hi(p):
                act.wait_ge(conv_step, 5 * (p + 1))
                A.copy(cv_hi[:, p], conv_b[:, p]).then_inc(conv_hi_done, 1)

            for n in range(3 * CT):
                p, which = divmod(n, 3)
                wait_output(act, ("conv", n))
                if n == 0:
                    act.wait_ge(score_step, n_dots)
                A.copy((conv_h, conv_c, conv_b)[which][:, p], psum(("conv", n))[:]).then_inc(freed(("conv", n)), 1)
                after(C_CONV + n)
                if n in (8, 11):
                    conv_hi((n - 8) // 3)
            for j in range(4):
                for n in range(2):
                    e = 2 * j + n
                    wait_output(act, ("gc", e))
                    if e < 2:
                        act.wait_ge(conv_step, 5 * e + 4)
                    if e >= 2:
                        act.wait_ge(bc_done, e - 1)
                    A.activation(conv_c[:, n], psum(("gc", e))[:], ACT.Sigmoid,
                                 bias=const[:, T_BIAS + DT + e:T_BIAS + DT + e + 1]).then_inc(freed(("gc", e)), 1)
                    after(C_GROUP + 3 * j + n)
                    if j == 0 and n == 0:
                        conv_hi(2)
                        conv_hi(3)
                for n in range(2):
                    e = 2 * j + n
                    wait_output(act, ("co", e))
                    if e >= 2:
                        act.wait_ge(bc_stored[e % 2], 16 * (e // 2))
                    A.copy(conv_c[:, 2 + n], psum(("co", e))[:]).then_inc(freed(("co", e)), 1)
                after(C_GROUP + 3 * j + 2)
            for p in range(PT_):
                wait_output(act, ("q", p))
                if p == 0:
                    for n in range(2):
                        act.wait_ge(bc_stored[n], 16 * DT // 2)
                A.copy(q_raw[:, p], psum(("q", p))[:]).then_inc(freed(("q", p)), 1)
                after(C_Q + p)
            for p in range(PT_):
                wait_output(act, ("k", p))
                if p >= 2:
                    act.wait_ge(k_lo_done, p - 1)
                A.copy(stage[:, p % 2], psum(("k", p))[:]).then_inc(k_staged, 1)
                A.copy(k_hi[:, p], psum(("k", p))[:]).then_inc(freed(("k", p)), 1)
                after(C_K + p)

            def v_split(p):
                wait_output(act, ("vt", p))
                src = psum(("vt", p))[:].rearrange("p (t c) -> p t c", c=P)
                if p:
                    act.wait_ge(v_lo_done, p)
                A.copy(stage[:, 1], psum(("vt", p))[:]).then_inc(v_staged, 1)
                A.copy(v_hi[:, :, p * P:(p + 1) * P], src).then_inc(freed(("vt", p)), 1)

            for p in range(PT_):
                wait_output(act, ("v", p))
                if p == 0:
                    act.wait_ge(k_lo_done, PT_)
                else:
                    wait_output(act, ("vt", p - 1))
                A.copy(stage[:, 0], psum(("v", p))[:]).then_inc(freed(("v", p)), 1)
                after(C_V + p)
                if p:
                    v_split(p - 1)
            for e in range(DT):
                if e == 1:
                    v_split(PT_ - 1)
                    act.wait_ge(v_lo_done, PT_)
                wait_output(act, ("ga", e))
                if e == 0:
                    wait_output(act, ("vt", PT_ - 1))
                if e >= 2:
                    act.wait_ge(ga_stored[e % 2], 16 * (e // 2))
                A.activation(stage[:, e % 2], psum(("ga", e))[:], ACT.Sigmoid,
                             bias=const[:, T_BIAS + e:T_BIAS + e + 1]).then_inc(freed(("ga", e)), 1)
                after(C_GA + e)

            def q_split(t):
                if t == 0:
                    wait_output(act, ("ga", DT - 1))
                else:
                    wait_output(act, s_names(PT_ * (t - 1))[-1])
                A.copy(qs_hi[:, t % 2], q_raw[:, :, t * P:(t + 1) * P]).then_inc(qs_hi_done, 1)

            def exponentials(w, a):
                t, p = divmod(w, PT_)
                x = probs[:, w % 2, a, 0:(t + 1) * P]
                if wide(w) or a == 1:
                    wait_evacuated(act, logits_of(w, a)[0])
                else:
                    act.wait_ge(first_max_done, w + 1)
                if t >= 2 and p == 0 and a == 0:
                    act.wait_ge(recip_done, t - 1)
                k, c = 2 * (w % 2) + a, 2 * p + a
                A.activation(x, x, ACT.Exp, scale=-1.0, bias=negmax[:, k:k + 1],
                             accum_out=sums[:, t % 2, c:c + 1]).then_inc(exp_done, 1)

            def probs_hi(name):
                w, src, place = transposed(name)
                wait_output(act, name)
                if w >= 2:
                    wait_output(act, ("o", w - 2))
                A.copy(place(pt_hi), src).then_inc(pt_hi_done, 1)

            def outputs(w):
                t, p = divmod(w, PT_)
                name = ("o", w)
                wait_output(act, name)
                cols = slice(t * P, (t + 1) * P)
                A.copy(q_raw[0:HD, p, cols], psum(name)[0:HD, 0:P])
                A.copy(q_raw[HD:P, p, cols], psum(name)[HD:P, P:2 * P]).then_inc(freed(name), 1)

            def reciprocals(t):
                wait_output(act, ("sums", t))
                if t >= 2:
                    act.wait_ge(at_scaled, t - 1)
                A.copy(rc_tok[:, t % 2].rearrange("p a b -> p (a b)"),
                       psum(("sums", t))[:, 0:PT_ * P]).then_inc(freed(("sums", t)), 1)

            q_split(0)
            exponentials(0, 0)
            exponentials(0, 1)
            for w in range(PAIRS + 2):
                if w >= 2:
                    outputs(w - 2)
                if w >= PT_ and w % PT_ == 1:
                    reciprocals(w // PT_ - 1)
                names = pt_names(w) if w < PAIRS else []
                for n in range(2):
                    if n < len(names):
                        probs_hi(names[n])
                    if w + 1 < PAIRS:
                        exponentials(w + 1, n)
                if w % PT_ == 0 and w // PT_ + 1 < ST:
                    q_split(w // PT_ + 1)
            act.wait_ge(at_scaled, ST)
            for p in range(PT_):
                A.copy(at_hi[:, p], q_raw[:, p]).then_inc(at_hi_done, 1)

            for e in range(DT):
                act.wait_ge(merged, e + 1)
                A.copy(mg_hi[:, e], stage[:, e % 2]).then_inc(mg_hi_done, 1)
                if e % 2:
                    after(C_AO + e // 2)

            def h_ready(e):
                wait_evacuated(act, ("wo", e))
                if e == 0:
                    act.wait_ge(mg_lo_done, DT)
            for d in range(DT):
                after_c = C_WO + d
                wait_output(act, ("wo", d))
                split(after_c + 2)
                h_ready(d)
                act.wait_ge(acc_done, DT + d - 1)
                A.activation(stage[:, d % 2], h[:, d], ACT.Square).then_inc(square_done, 1)
            act.wait_ge(var_done, 2)
            A.activation(small[:, 8:16], small[:, 0:8], ACT.Sqrt).then_inc(sqrt_done, 1)
            norm_split(1, xm_hi)

            def tap2(g, m, col, more=0, laps=0, wait_slot=True):
                wait_output(act, ("up", g, m), more)
                A.activation(ff_t[:, m], psum(("up", g, m))[:], ACT.Copy, scale=const[:, col]).then_inc(tap2_done, 1)

            def ffn_group(g, c, first=False, i=None):
                j = 0 if i is None else i
                lap = i
                groups = g + 2 * j
                for m in range(4):
                    if not first and m in (1, 3):
                        act.wait_ge(u_lo_done, 2 * groups - 1 + m // 2)
                    if not first and m in (0, 2):
                        act.wait_ge(silu_done, 2 * groups - 1 + m // 2)
                    col = T_FCONV + 12 * g + 3 * m + 2
                    col = slice(col, col + 1) if i is None else ds(col + 24 * i, 1)
                    tap2(g, m, col, 24 * j)
                    split(c + m + 2, lap)
                    if m in (1, 3):
                        if not first:
                            act.wait_ge(ff_done, 2 * groups - 1 + m // 2)
                        wait_evacuated(act, ("up", g, m - 1), 6 * j)
                        A.activation(stage[:, m // 2], ff_t[:, m - 1], ACT.Silu).then_inc(silu_done, 1)
                    if m == 2:
                        ffn_hi(g, 0, groups, j)

            def ffn_hi(g, a, groups, j):
                act.wait_ge(ff_done, 2 * groups + a + 1)
                A.copy(u_hi[:, g % 2, a], ff_t[:, 2 * a + 1]).then_inc(u_hi_done, 1)

            ffn_group(0, C_FF, first=True)
            ffn_hi(0, 1, 0, 0)
            with act.Fori(0, 5) as i:
                for n in range(2):
                    g = 1 + n
                    ffn_group(g, C_FF + 4 + 6 * n, i=i)
                    ffn_hi(g, 1, g + 2 * i, i)
                    for k in range(2):
                        wait_output(act, ("dn", n, 4 * k + 3), 24 * i)
                        c = C_FF + 8 + 6 * n + k
                        split(c + 2, i)
            for d in range(DT):
                wait_evacuated(act, ("dn", FT // 2 - 1, d))
                act.wait_ge(acc_done, 2 * DT + d - 1)
                A.activation(stage[:, d % 2], h[:, d], ACT.Square).then_inc(square_done, 1)
            act.wait_ge(var_done, 3)
            A.activation(small[:, 8:16], small[:, 0:8], ACT.Sqrt).then_inc(sqrt_done, 1)

        @block.gpsimd
        def _(pool):
            G_ = nc.gpsimd

            def lo(c, lap=None):
                pool.wait_ge(w_hi_done, c + 1 + (0 if lap is None else 12 * lap))
                G_.tensor_tensor(w_lo[:, c % 2], w_raw[:, c % 3], w_hi[:, c % 2].bitcast(f32),
                                 ALU.subtract).then_inc(w_lo_done, 1)

            G_.memset(ident[:], 0.0).then_inc(ident_zero, 1)
            G_.memset(ones[:], 1.0).then_inc(fixed_ready, 1)
            G_.memset(mask[:, 0:mask_at(2)], 0.0).then_inc(ident_zero, 1)
            pool.wait_ge(ident_zero, 2)
            G_.affine_select(out=ident[:], in_=ident[:], compare_op=ALU.not_equal, fill=1.0, base=0,
                             pattern=[[-1, P]], channel_multiplier=1).then_inc(fixed_ready, 1)
            for t in range(2):
                diag = mask[:, mask_at(t) + t * P:mask_at(t + 1)]
                last = G_.affine_select(out=diag, in_=diag, compare_op=ALU.is_ge, fill=MASKED, base=0,
                                        pattern=[[-1, P]], channel_multiplier=1)
            last.then_inc(fixed_ready, 1)
            for c in range(C_CONV + 2):
                lo(c)
            for t in range(2, ST):
                pool.wait_ge(score_step, NH * (t - 1))
                diag = mask[:, mask_at(t) + t * P:mask_at(t + 1)]
                G_.affine_select(out=diag, in_=diag, compare_op=ALU.is_ge, fill=ACAUSAL, base=0,
                                 pattern=[[-1, P]], channel_multiplier=1).then_inc(causal_done, 1)
            for c in range(C_CONV + 2, C_GROUP + 4):
                lo(c)
                if c in (C_CONV + 10, C_CONV + 13, C_GROUP + 2):
                    for p in {C_CONV + 10: (0,), C_CONV + 13: (1,), C_GROUP + 2: (2, 3)}[c]:
                        pool.wait_ge(conv_hi_done, p + 1)
                        G_.tensor_tensor(cv_lo[:, p], conv_b[:, p], cv_hi[:, p].bitcast(f32),
                                         ALU.subtract).then_inc(conv_lo_done, 1)
            for j in range(4):
                lo(C_GROUP + 3 * j + 4)
                for n in range(2):
                    e = 2 * j + n
                    wait_evacuated(pool, ("gc", e))
                    wait_evacuated(pool, ("co", e))
                    G_.tensor_tensor(conv_c[:, 2 + n], conv_c[:, 2 + n], conv_c[:, n],
                                     ALU.mult).then_inc(bc_done, 1)
                if j < 3:
                    lo(C_GROUP + 3 * j + 5)
                    lo(C_GROUP + 3 * j + 6)
            for c in range(C_GROUP + 14, C_K + 2):
                lo(c)
            for p in range(PT_):
                lo(C_K + p + 2)
                pool.wait_ge(k_staged, p + 1)
                wait_evacuated(pool, ("k", p))
                G_.tensor_tensor(k_lo[:, p], stage[:, p % 2], k_hi[:, p].bitcast(f32),
                                 ALU.subtract).then_inc(k_lo_done, 1)

            def v_lo_part(p):
                pool.wait_ge(v_staged, p + 1)
                wait_evacuated(pool, ("vt", p))
                G_.tensor_tensor(v_lo[:, :, p * P:(p + 1) * P],
                                 stage[:, 1].rearrange("p (t c) -> p t c", c=P),
                                 v_hi[:, :, p * P:(p + 1) * P].bitcast(f32), ALU.subtract).then_inc(v_lo_done, 1)

            for p in range(PT_):
                lo(C_V + p + 2)
                if p:
                    v_lo_part(p - 1)
            lo(C_GA + 2)
            v_lo_part(PT_ - 1)
            for c in range(C_GA + 3, C_AO + 2):
                lo(c)
            def widen(t):
                pool.wait_ge(recip_done, t + 1)
                if t >= 2:
                    wait_output(pool, ("sums", t - 2))
                G_.tensor_copy(rc_wide[:, t % 2].rearrange("p a (b c) -> p (a b) c", c=HD),
                               recips[:, t % 2].unsqueeze(2).to_broadcast([P, NH, HD])).then_inc(rc_widened, 1)

            def scale_outputs(t):
                wait_evacuated(pool, ("sums", t))
                for p in range(PT_):
                    wait_evacuated(pool, ("o", PT_ * t + p))
                x = q_raw[:, :, t * P:(t + 1) * P]
                G_.tensor_tensor(x, x, rc_tok[:, t % 2], ALU.mult).then_inc(at_scaled, 1)

            for t in range(ST):
                widen(t)
                if t:
                    scale_outputs(t - 1)
            scale_outputs(ST - 1)
            for c in range(C_AO + 2, C_FF + 6):
                lo(c)

            def u_lo_part(g, a, n):
                pool.wait_ge(u_hi_done, n)
                G_.tensor_tensor(u_lo[:, g % 2, a], ff_t[:, 2 * a + 1], u_hi[:, g % 2, a].bitcast(f32),
                                 ALU.subtract).then_inc(u_lo_done, 1)

            u_lo_part(0, 0, 1)
            u_lo_part(0, 1, 2)
            with pool.Fori(0, 5) as i:
                for n in range(2):
                    g = 1 + n
                    for m in range(6):
                        lo(C_FF + 6 + 6 * n + m, i)
                        if m == 2:
                            u_lo_part(g, 0, 4 * i + 2 * g + 1)
                        if m == 3:
                            u_lo_part(g, 1, 4 * i + 2 * g + 2)

        @block.vector
        def _(dve):
            V = nc.vector

            steps = {}

            def step(s, ins):
                steps[s.name] = steps.get(s.name, 0) + 1
                ins.then_inc(s, 1)
                dve.wait_ge(s, steps[s.name])

            def accumulate(n, d):
                dve.wait_ge(square_done, DT * n + d + 1)
                if DT * n + d:
                    dve.wait_ge(acc_done, DT * n + d)
                if d == 0:
                    if n:
                        wait_output(dve, f"n{n - 1}_sum")
                    V.tensor_copy(nrm_acc[:], stage[:, 0]).then_inc(acc_done, 1)
                else:
                    V.tensor_tensor(nrm_acc[:], nrm_acc[:], stage[:, d % 2], ALU.add).then_inc(acc_done, 1)

            def norm_rms(n):
                v, s, y, t = small[:, 0:8], small[:, 8:16], small[:, 16:24], small[:, 24:32]
                a = f"n{n}_sum"
                wait_output(dve, a)
                if n:
                    dve.wait_ge(diag_done, n)
                V.tensor_scalar(v, psum(a)[:, 0:ST], 1.0 / D, EPS, ALU.mult, ALU.add).then_inc(freed(a), 1)
                wait_evacuated(dve, a)
                V.tensor_copy(t, v).then_inc(var_done, 1)
                dve.wait_ge(sqrt_done, n + 1)
                step(newton, V.reciprocal(y, s))
                step(newton, V.tensor_tensor(t, y, y, ALU.mult))
                step(newton, V.tensor_tensor(t, t, v, ALU.mult))
                step(newton, V.tensor_scalar(t, t, -0.5, 1.5, ALU.mult, ALU.add))
                step(newton, V.tensor_tensor(y, y, t, ALU.mult))
                if n == 0:
                    dve.wait_ge(fixed_ready, 3)
                else:
                    wait_output(dve, f"n{n - 1}_bc")
                for t in range(ST):
                    last = V.tensor_scalar(nrm_diag[:, t], ident[:], y[:, t:t + 1], None, ALU.mult)
                last.then_inc(diag_done, 1)

            def norm_scale(n, src, g0, hi, lo_):
                b = f"n{n}_bc"
                wait_output(dve, b)

                def low(d):
                    dve.wait_ge(norm_hi, DT * n + d + 1)
                    V.tensor_tensor(lo_[:, d], nrm_x[:, d % 2], hi[:, d].bitcast(f32),
                                    ALU.subtract).then_inc(norm_lo, 1)

                for d in range(DT):
                    if DT * n + d >= 2:
                        dve.wait_ge(norm_lo, DT * n + d - 1)
                    V.scalar_tensor_tensor(nrm_x[:, d % 2], src[:, d], const[:, g0 + d:g0 + d + 1],
                                           psum(b)[:], ALU.mult, ALU.mult).then_inc(scaled_done, 1)
                    if d:
                        low(d - 1)
                low(DT - 1)
                if n:
                    wait_evacuated(dve, f"n{n - 1}_bc")
                V.tensor_copy(small[:, 32:33], psum(b)[:, 0:1]).then_inc(freed(b), 1)

            dve.wait_ge(const_in, 16)
            for d in range(DT):
                accumulate(0, d)
            norm_rms(0)
            norm_scale(0, x_in, T_GMIX, xn_hi, xn_lo)
            dve.wait_ge(ik_hi_done, 1)
            wait_output(dve, "ikw")
            dve.wait_ge(iw_copied, 1)
            V.tensor_tensor(ik_lo[0:HD], psum("ikw")[0:HD], ik_hi[0:HD].bitcast(f32),
                            ALU.subtract).then_inc(freed("ikw"), 1)
            for p in range(PT_):
                dve.wait_ge(iq_hi_done, p + 1)
                V.tensor_tensor(iq_lo[:, p], psum(("iq", p))[:], iq_hi[:, p].bitcast(f32),
                                ALU.subtract).then_inc(freed(("iq", p)), 1)
            wait_output(dve, "iw_tok")
            V.tensor_copy(iw_tok[:].rearrange("p t h -> p (t h)"), psum("iw_tok")[:, 0:ST * NH]).then_inc(freed("iw_tok"), 1)
            wait_evacuated(dve, "iw_tok")
            n_dots = 0
            for t in range(2, ST):
                score = mask[:, mask_at(t):mask_at(t + 1)]
                n = (t + 1) * P
                for hh in range(NH):
                    wait_evacuated(dve, ("dots", t, hh))
                    r = rel[:, n_dots % 2, 0:n]
                    w = iw_tok[:, t, hh:hh + 1]
                    if hh == 0:
                        step(score_step, V.tensor_scalar(score, r, w, None, ALU.mult))
                    else:
                        step(score_step, V.scalar_tensor_tensor(score, r, w, score, ALU.mult, ALU.add))
                    n_dots += 1

            done_rounds = [0]

            def topk_rounds(t, rounds):
                score = mask[:, mask_at(t):mask_at(t + 1)]
                first = 2 * done_rounds[0]
                if first == 0:
                    dve.wait_ge(causal_done, ST - 2)
                for r in range(rounds):
                    if first or r:
                        dve.wait_ge(topk_step, first + 2 * r)
                    V.max(top8[:], score).then_inc(topk_step, 1)
                    dve.wait_ge(topk_step, first + 2 * r + 1)
                    V.match_replace(score, top8[:], score, TAKEN).then_inc(topk_step, 1)
                done_rounds[0] += rounds
                dve.wait_ge(topk_step, 2 * done_rounds[0])

            def choose(t):
                score = mask[:, mask_at(t):mask_at(t + 1)]
                V.tensor_scalar(score, score, UNCHOSEN, MASKED, ALU.is_gt, ALU.mult).then_inc(mask_done, 1)

            def convolve(p):
                for n in range(3):
                    wait_evacuated(dve, ("conv", 3 * p + n))

                def tap(k):
                    return const[:, T_CONV + k * CT + p:T_CONV + k * CT + p + 1]

                u, y, b = conv_c[:, p], conv_h[:, p], conv_b[:, p]
                step(conv_step, V.tensor_tensor(u, u, y, ALU.mult))
                step(conv_step, V.tensor_scalar(y, u, tap(2), None, ALU.mult))
                step(conv_step, V.scalar_tensor_tensor(y[:, 1:S], u[:, 0:S - 1], tap(1), y[:, 1:S], ALU.mult, ALU.add))
                step(conv_step, V.scalar_tensor_tensor(y[:, 2:S], u[:, 0:S - 2], tap(0), y[:, 2:S], ALU.mult, ALU.add))
                step(conv_step, V.tensor_tensor(b, b, y, ALU.mult))

            ROUNDS = TOPK // 8
            topk_rounds(2, ROUNDS)
            choose(2)
            convolve(0)
            topk_rounds(3, ROUNDS)
            choose(3)
            convolve(1)
            topk_rounds(4, 20)
            convolve(2)
            convolve(3)
            topk_rounds(4, ROUNDS - 20)
            choose(4)
            for t in range(5, ST):
                topk_rounds(t, ROUNDS)
                choose(t)
            dve.wait_ge(mask_done, ST - 2)

            def q_split(t):
                dve.wait_ge(qs_hi_done, t + 1)
                V.tensor_tensor(qs_lo[:, t % 2], q_raw[:, :, t * P:(t + 1) * P], qs_hi[:, t % 2].bitcast(f32),
                                ALU.subtract).then_inc(qs_lo_done, 1)

            def masked_max(w, a):
                t = w // PT_
                n = (t + 1) * P
                name, cols = logits_of(w, a)
                wait_output(dve, name)
                if w >= 2:
                    wait_output(dve, pt_names(w - 2)[a if wide(w - 2) else 0])
                k = 2 * (w % 2) + a
                ins = V.tensor_tensor_reduce(out=probs[:, w % 2, a, 0:n], in0=psum(name)[:, cols],
                                             in1=mask[:, mask_at(t):mask_at(t + 1)], scale=-scale, scalar=3e38,
                                             op0=ALU.add, op1=ALU.min, accum_out=negmax[:, k:k + 1])
                if wide(w) or a == 1:
                    ins.then_inc(freed(name), 1)
                else:
                    ins.then_inc(first_max_done, 1)

            def probs_lo(name):
                w, src, place = transposed(name)
                dve.wait_ge(pt_hi_done, pt_number[name])
                V.tensor_tensor(place(pt_lo), src, place(pt_hi).bitcast(f32), ALU.subtract).then_inc(freed(name), 1)

            q_split(0)
            for w in range(2):
                for a in range(2):
                    masked_max(w, a)
            for w in range(PAIRS):
                t, p = divmod(w, PT_)
                if p == PT_ - 1:
                    dve.wait_ge(exp_done, NH * (t + 1))
                    if t >= 2:
                        dve.wait_ge(rc_widened, t - 1)
                    V.reciprocal(recips[:, t % 2], sums[:, t % 2]).then_inc(recip_done, 1)
                for a in range(2):
                    if a < len(pt_names(w)):
                        probs_lo(pt_names(w)[a])
                    if w + 2 < PAIRS:
                        masked_max(w + 2, a)
                if p == 0 and t + 1 < ST:
                    q_split(t + 1)
            for p in range(PT_):
                dve.wait_ge(at_hi_done, p + 1)
                V.tensor_tensor(at_lo[:, p], q_raw[:, p], at_hi[:, p].bitcast(f32), ALU.subtract).then_inc(at_lo_done, 1)

            def merge_lo(e):
                dve.wait_ge(mg_hi_done, e + 1)
                V.tensor_tensor(mg_lo[:, e], stage[:, e % 2], mg_hi[:, e].bitcast(f32),
                                ALU.subtract).then_inc(mg_lo_done, 1)

            for e in range(DT):
                wait_output(dve, ("ao", e))
                if e >= 2:
                    dve.wait_ge(mg_lo_done, e - 1)
                dve.wait_ge(gate_loaded[e % 2], 32 * (e // 2 + 1))
                V.tensor_tensor(stage[:, e % 2], psum(("ao", e))[:], gate_in[:, e % 2, 0],
                                ALU.mult).then_inc(freed(("ao", e)), 1)
                wait_evacuated(dve, ("ao", e))
                V.tensor_tensor(stage[:, e % 2], stage[:, e % 2], gate_in[:, e % 2, 1], ALU.add).then_inc(merged, 1)
                if e:
                    merge_lo(e - 1)
            merge_lo(DT - 1)

            def add_to_h(name, e, more=0):
                wait_output(dve, name, more)
                V.tensor_tensor(h[:, e], psum(name)[:], h[:, e], ALU.add).then_inc(freed(name), 1)

            for e in range(DT):
                dve.wait_ge(x_loaded[e], 32)
                add_to_h(("wo", e), e)
                if e:
                    accumulate(1, e - 1)
            accumulate(1, DT - 1)
            norm_rms(1)
            norm_scale(1, h, T_GFFN, xm_hi, xm_lo)

            def conv_taps(g, m, groups, i=None):
                j = 0 if i is None else i
                base_col = T_FCONV + 12 * g + 3 * m

                def tap(k):
                    return const[:, base_col + k:base_col + k + 1] if i is None else const[:, ds(base_col + k + 24 * i, 1)]

                t, src = ff_t[:, m], psum(("up", g, m))
                dve.wait_ge(tap2_done, 4 * groups + m + 1)
                V.scalar_tensor_tensor(t[:, 1:S], src[:, 0:S - 1], tap(1), t[:, 1:S], ALU.mult,
                                       ALU.add).then_inc(tap1_done, 1)
                dve.wait_ge(tap1_done, 4 * groups + m + 1)
                V.scalar_tensor_tensor(t[:, 2:S], src[:, 0:S - 2], tap(0), t[:, 2:S], ALU.mult,
                                       ALU.add).then_inc(freed(("up", g, m)), 1)

            def gate_times_value(g, a, groups, i=None):
                j = 0 if i is None else i
                dve.wait_ge(silu_done, 2 * groups + a + 1)
                wait_evacuated(dve, ("up", g, 2 * a + 1), 6 * j)
                V.tensor_tensor(ff_t[:, 2 * a + 1], ff_t[:, 2 * a + 1], stage[:, a], ALU.mult).then_inc(ff_done, 1)

            def ffn_group(g, i=None):
                groups = g if i is None else g + 2 * i
                conv_taps(g, 0, groups, i)
                conv_taps(g, 1, groups, i)
                gate_times_value(g, 0, groups, i)
                conv_taps(g, 2, groups, i)
                conv_taps(g, 3, groups, i)
                gate_times_value(g, 1, groups, i)

            ffn_group(0)
            with dve.Fori(0, 5) as i:
                for n in range(2):
                    ffn_group(1 + n, i)
                    for e in range(DT):
                        add_to_h(("dn", n, e), e, 24 * i)
            for e in range(DT):
                add_to_h(("dn", FT // 2 - 1, e), e)
                if e:
                    accumulate(2, e - 1)
            accumulate(2, DT - 1)
            norm_rms(2)
            wait_output(dve, "n2_bc")
            for d in range(DT):
                if d >= 2:
                    dve.wait_ge(out_stored[d % 2], 16 * (d // 2))
                elif d == 0:
                    dve.wait_ge(norm_lo, 2 * DT)
                V.scalar_tensor_tensor(nrm_x[:, d % 2], h[:, d], const[:, T_GFIN + d:T_GFIN + d + 1],
                                       psum("n2_bc")[:], ALU.mult, ALU.mult).then_inc(out_scaled, 1)


def pack(w_in, w_attn_out, w_conv_out, w_o, w_up, w_down):
    def cols(w, c0):
        return w[:, c0:c0 + P].reshape(-1, P, P).transpose(1, 0, 2)

    ikw = np.zeros((D, P), w_in.dtype)
    ikw[:, 0:HD] = w_in[:, IK0:IK0 + HD]
    ikw[:, HD:HD + NH] = w_in[:, IW0:IW0 + NH]
    out = [cols(ikw, 0)]
    out += [cols(w_in, IQ0 + p * P) for p in range(PT_)]
    for p in range(CT):
        out += [cols(w_in, c + p * P) for c in (CH0, CC0, CB0)]

    def two(w, j):
        return np.concatenate([cols(w, (2 * j) * P), cols(w, (2 * j + 1) * P)], axis=1)

    for j in range(4):
        out += [cols(w_in, G0 + D + (2 * j + n) * P) for n in range(2)] + [two(w_conv_out, j)]
    for c in (Q0, K0, V0):
        out += [cols(w_in, c + p * P) for p in range(PT_)]
    out += [cols(w_in, G0 + e * P) for e in range(DT)]
    out += [two(w_attn_out, j) for j in range(4)]
    out += [cols(w_o, e * P) for e in range(DT)]

    def up(g):
        return [cols(w_up, c) for a in range(2) for c in ((2 * g + a) * P, FF + (2 * g + a) * P)]

    def down(g):
        rows = w_down[2 * g * P:(2 * g + 2) * P]
        return [np.concatenate([cols(rows, (4 * n + e) * P) for e in range(4)], axis=1) for n in range(2)]

    out += up(0)
    for g in range(1, FT // 2):
        out += up(g) + down(g - 1)
    out += down(FT // 2 - 1)
    return np.ascontiguousarray(np.stack(out).reshape(N_CHUNKS, P, 8 * P))


def kernel(**inputs):
    import concourse.bacc as bacc
    from concourse.bass_utils import run_bass_kernel_spmd

    a = {k: np.asarray(v) for k, v in inputs.items()}
    x = a["x"]
    xT = np.ascontiguousarray(x[0].T.reshape(DT, P, S))
    wts = pack(a["w_in"][0], a["w_attn_out"][0], a["w_conv_out"][0], a["w_o"][0], a["w_up"][0], a["w_down"][0])

    def per_channel(v):
        return v.reshape(-1, P).T

    fconv = a["ffn_conv_w"][0].reshape(3, 2, FT // 2, 2, P)
    consts = np.ascontiguousarray(np.concatenate([
        per_channel(a["norm_mix_g"][0]), per_channel(a["norm_ffn_g"][0]), per_channel(a["norm_final_g"]),
        per_channel(a["b_gate"][0]), per_channel(a["conv_w"][0].reshape(-1)),
        fconv.transpose(4, 2, 3, 1, 0).reshape(P, -1)], axis=1))
    arrays = {"xT_dram": xT, "wts_dram": wts, "consts_dram": consts}

    nc = bacc.Bacc("TRN2", target_bir_lowering=False, num_devices=1)
    f32 = mybir.dt.float32
    ins = [nc.dram_tensor(n, v.shape, f32, kind="ExternalInput").ap() for n, v in arrays.items()]
    out = nc.dram_tensor("outT_dram", (DT, P, S), f32, kind="ExternalOutput").ap()
    bc_dram = nc.dram_tensor("bc_dram", (DT, P, S), f32, kind="Internal").ap()
    ga_dram = nc.dram_tensor("ga_dram", (DT, P, S), f32, kind="Internal").ap()
    build(nc, *ins, out, bc_dram, ga_dram)
    r = run_bass_kernel_spmd(nc, [arrays], core_ids=[0])
    got = np.asarray(r.results[0]["outT_dram"])
    return np.ascontiguousarray(got.reshape(D, S).T).reshape(x.shape)
```

```python
from contextlib import ExitStack, contextmanager

import numpy as np

import concourse.bass as bass
from concourse import mybir

P = 128
D = 1024
S = 1024
DT = D // P
ST = S // P
NH = 8
HD = 64
PT_ = NH * HD // P
CW = 512
CT = CW // P
FF = 2816
FT = FF // P
TOPK = 256
EPS = 1e-6
HALF = 512

Q0, K0, V0 = 0, 512, 1024
IQ0, IK0, IW0 = 1536, 2048, 2112
CH0, CB0, CC0, G0 = 2120, 2632, 3144, 3656

PAIRS = ST * PT_

C_IKW = 0
C_IQ = 1
C_CONV = 5
C_GROUP = 17
C_Q = 29
C_K = 33
C_V = 37
C_GA = 41
C_AO = 49
C_WO = 53
C_FF = 61
N_CHUNKS = 127

T_GMIX, T_GFFN, T_GFIN, T_BIAS = 0, 8, 16, 24
T_CONV = 40
T_FCONV = T_CONV + 3 * CT
N_CONST = T_FCONV + 3 * 2 * FT

TAKEN = -3e38
ACAUSAL = -1e38
UNCHOSEN = -2e38
MASKED = -1e30


def mask_at(t):
    return P * t * (t + 1) // 2


def wide(w):
    return w // PT_ >= 4


def s_names(w):
    return [("s", w, 0), ("s", w, 1)] if wide(w) else [("s", w)]


def pt_names(w):
    return [("pt", w, 0), ("pt", w, 1)] if wide(w) else [("pt", w)]


DOTS = [(t, h) for t in range(2, ST) for h in range(NH)]
DOTS_BEFORE = [[0, 1, 1, 1, 1, 1, 1, 2], *[[1] * DT] * 5]
MIXED = len(DOTS_BEFORE)
assert sum(map(sum, DOTS_BEFORE)) == len(DOTS)


def dots_before(n, k=None):
    if n >= MIXED:
        return []
    if k is None:
        return [d for j in range(DT) for d in dots_before(n, j)]
    first = sum(map(sum, DOTS_BEFORE[:n])) + sum(DOTS_BEFORE[n][:k])
    return DOTS[first:first + DOTS_BEFORE[n][k]]


def tickets():
    order = ["ikw", ("iq", 0), "n0_sum", "n0_bc", ("iq", 1), ("iq", 2), "iw_tok", ("iq", 3)]
    for n in range(3 * CT):
        order += [("dots", *d) for d in dots_before(n)] + [("conv", n)]
    for j in range(4):
        order += [("gc", 2 * j), ("gc", 2 * j + 1), ("co", 2 * j), ("co", 2 * j + 1)]
    order += [("q", p) for p in range(PT_)] + [("k", p) for p in range(PT_)]
    order += [("v", 0)]
    for p in range(1, PT_):
        order += [("v", p), ("vt", p - 1)]
    order += [("ga", 0), ("vt", PT_ - 1)] + [("ga", e) for e in range(1, DT)]
    order += s_names(0) + s_names(1)
    for w in range(PAIRS + 1):
        t, p = divmod(w, PT_)
        a, b = (pt_names(w) if w < PAIRS else []), (s_names(w + 2) if w + 2 < PAIRS else [])
        order += a[:1] + b[:1] + a[1:] + b[1:]
        if w >= 1:
            order += [("o", w - 1)]
        if (w >= 1 and p == 0 and w < PAIRS) or w == PAIRS - 1:
            order += [("sums", t if w == PAIRS - 1 else t - 1)]
    order += [("ao", e) for e in range(DT)] + [("wo", e) for e in range(DT)]
    order += [("up", 0, 0), "n1_sum", ("up", 0, 1), "n1_bc", ("up", 0, 2), ("up", 0, 3)]
    for g in range(1, FT // 2):
        order += [("up", g, m) for m in range(4)] + [("dn", g - 1, e) for e in range(DT)]
    order += [("dn", FT // 2 - 1, e) for e in range(DT)]
    order += ["n2_sum", "n2_bc"]
    return {name: n for n, name in enumerate(order)}


def places(numbers):
    where, held, turn = {}, [0] * 4, 0
    for name in numbers:
        if name[0] == "conv" and name[1] < MIXED:
            pair = name[1] % 2
            turn = 1 - pair
        elif name[0] == "dots":
            pair = 2 + name[2] % 2
        else:
            pair, turn = turn, (turn + 1) % 4
        held[pair] += 1
        where[name] = (pair, held[pair])
    return where


def build(nc, xT, wts, consts, outT, bc_dram, ga_dram):
    f32, f32r = mybir.dt.float32, mybir.dt.float32r
    ALU, ACT = mybir.AluOpType, mybir.ActivationFunctionType
    ds = bass.ds
    U = tickets()
    PLACE = places(U)
    scale = float(HD) ** -0.5
    iw_scale = float(NH) ** -0.5 * float(HD) ** -0.5

    KB = 1024
    base = 16512
    X = base
    Q = X + 64 * KB
    M = Q + 80 * KB
    W = M + 18 * KB
    G = W + 28 * KB
    Z = G + 8 * KB

    def at(name, shape, dt, where):
        return nc.alloc_sbuf_tensor_at(name, [P, *shape], dt, offset=where)

    w_raw = at("w_raw", [3, 8, P], f32, W)
    w_hi = at("w_hi", [2, 8, P], f32r, W + 12 * KB)
    w_lo = at("w_lo", [2, 8, P], f32r, W + 20 * KB)
    stage = at("stage", [2, S], f32, G)
    const = at("const", [N_CONST], f32, Z)
    ident = at("ident", [P], f32, Z + 1024)
    ones = at("ones", [P], f32, Z + 1536)
    small = at("small", [64], f32, Z + 2048)
    iw_tok = at("iw_tok", [ST, NH], f32, Z + 2304)
    negmax = at("negmax", [4], f32, Z + 2560)
    sums = at("sums", [2, NH], f32, Z + 2592)
    top8 = at("top8", [8], f32, Z + 2656)
    recips = at("recips", [2, NH], f32, Z + 2688)

    nrm_acc = at("nrm_acc", [S], f32, Z + 3 * KB)
    xn_hi = at("xn_hi", [DT, S], f32r, X)
    xn_lo = at("xn_lo", [DT, S], f32r, X + 32 * KB)
    x_in = at("x_in", [DT, S], f32, Q)
    nrm_wide = [at("nrm_wide0", [ST, P], f32, M + 2 * KB), at("nrm_wide1", [ST, P], f32, Q + 60 * KB)]
    rrms = [at("rrms0", [S], f32, M + 6 * KB), at("rrms1", [S], f32, Q + 56 * KB)]
    iq_raw = at("iq_raw", [2, S], f32, M + 10 * KB)
    iq_both = at("iq_both", [NH, S], f32r, Q + 48 * KB)
    iq_lo = at("iq_lo", [2, S], f32r, Q + 32 * KB)
    ik_hi = at("ik_hi", [S], f32r, Q + 40 * KB)
    ik_lo = at("ik_lo", [S], f32r, Q + 44 * KB)
    rel = at("rel", [2, S], f32, G)
    conv_h = at("conv_h", [CT, S], f32, Q)
    conv_c = at("conv_c", [CT, S], f32, Q + 16 * KB)
    conv_b = at("conv_b", [CT, S], f32, Q + 32 * KB)
    cv_hi = at("cv_hi", [CT, S], f32r, Q + 48 * KB)
    cv_lo = at("cv_lo", [CT, S], f32r, Q + 64 * KB)
    q_raw = at("q_raw", [PT_, S], f32, Q)
    k_hi = at("k_hi", [PT_, S], f32r, Q + 16 * KB)
    k_lo = at("k_lo", [PT_, S], f32r, Q + 32 * KB)
    v_hi = at("v_hi", [ST, NH * HD], f32r, Q + 48 * KB)
    v_lo = at("v_lo", [ST, NH * HD], f32r, Q + 64 * KB)
    mask = at("mask", [ST * (ST + 1) // 2 * P], f32, M)
    probs = at("probs", [2, 2, S], f32, X)
    qs_hi = at("qs_hi", [2, PT_, P], f32r, X + 16 * KB)
    qs_lo = at("qs_lo", [2, PT_, P], f32r, X + 20 * KB)
    rc_wide = at("rc_wide", [2, PT_, P], f32, X + 24 * KB)
    rc_tok = at("rc_tok", [2, PT_, P], f32, X + 28 * KB)
    pt_hi = at("pt_hi", [2, ST, 2, P], f32r, X + 32 * KB)
    pt_lo = at("pt_lo", [2, ST, 2, P], f32r, X + 48 * KB)
    at_hi = at("at_hi", [PT_, S], f32r, X + 32 * KB)
    at_lo = at("at_lo", [PT_, S], f32r, X + 48 * KB)
    gate_in = at("gate_in", [2, 2, S], f32, M)
    mg_hi = at("mg_hi", [DT, S], f32r, Q)
    mg_lo = at("mg_lo", [DT, S], f32r, Q + 32 * KB)
    h = at("h", [DT, S], f32, X)
    xm_hi = at("xm_hi", [DT, S], f32r, X + 32 * KB)
    xm_lo_parts = [at("xm_lo0", [4, S], f32r, Q + 64 * KB), at("xm_lo1", [4, S], f32r, M)]
    up_out = at("up_out", [2, S], f32, Q)
    ff_t = at("ff_t", [4, S], f32, Q + 8 * KB)
    u_hi = at("u_hi", [2, 2, S], f32r, Q + 24 * KB)
    u_lo = at("u_lo", [2, 2, S], f32r, Q + 40 * KB)
    result = at("result", [DT, S], f32, Q)

    ctx = ExitStack()
    with ctx:
        pair = [ctx.enter_context(nc.psum_tensor(f"pair{i}", [P, S], f32)) for i in range(4)]

        def sem(name):
            return ctx.enter_context(nc.semaphore(name))

        const_in = sem("const_in")
        x_loaded = [sem(f"x_loaded{d}") for d in range(DT)]
        w_loaded = [sem(f"w_loaded{s}") for s in range(3)]
        w_hi_done, w_lo_done = sem("w_hi_done"), sem("w_lo_done")
        out_ready = sem("out_ready")
        evacuated = [sem(f"evacuated{i}") for i in range(4)]
        fixed_ready, ident_zero = sem("fixed_ready"), sem("ident_zero")
        square_done, acc_done, newton = sem("square_done"), sem("acc_done"), sem("newton")
        var_done, sqrt_done, wide_done = sem("var_done"), sem("sqrt_done"), sem("wide_done")
        gained_hi, gained_lo, gained_used = sem("gained_hi"), sem("gained_lo"), sem("gained_used")
        x_scaled, xn_hi_done = sem("x_scaled"), sem("xn_hi_done")
        xn_lo_done = {"dve": sem("xn_lo_done_dve"), "pool": sem("xn_lo_done_pool")}
        iq_moved = [[sem(f"iq{p}_{what}_moved") for what in ("odd_hi", "odd_lo", "even_lo")] for p in range(PT_)]
        idx_scaled, idx_lo_done = sem("idx_scaled"), sem("idx_lo_done")
        ik_hi_done = sem("ik_hi_done")
        ik_copied = [sem("ik_hi_copied"), sem("ik_lo_copied")]
        iq_hi_done = sem("iq_hi_done")
        score_step, causal_done = sem("score_step"), sem("causal_done")
        topk_step, mask_done = sem("topk_step"), sem("mask_done")
        conv_step, conv_hi_done, conv_lo_done = sem("conv_step"), sem("conv_hi_done"), sem("conv_lo_done")
        gc_done, co_copied, bc_done = sem("gc_done"), sem("co_copied"), sem("bc_done")
        bc_stored = [sem("bc_stored0"), sem("bc_stored1")]
        ga_stored = [sem("ga_stored0"), sem("ga_stored1")]
        k_staged, k_lo_done, v_staged, v_lo_done = sem("k_staged"), sem("k_lo_done"), sem("v_staged"), sem("v_lo_done")
        qs_hi_done, qs_lo_done = sem("qs_hi_done"), sem("qs_lo_done")
        first_max_done = sem("first_max_done")
        exp_done, recip_done = sem("exp_done"), sem("recip_done")
        rc_widened, at_scaled = sem("rc_widened"), sem("at_scaled")
        pt_hi_done, at_hi_done, at_lo_done = sem("pt_hi_done"), sem("at_hi_done"), sem("at_lo_done")
        gate_loaded = [sem("gate_loaded0"), sem("gate_loaded1")]
        merged, mg_hi_done, mg_lo_done = sem("merged"), sem("mg_hi_done"), sem("mg_lo_done")
        first_up_copied, first_up_scaled = sem("first_up_copied"), sem("first_up_scaled")
        tap2_done, tap1_done, tap0_done = sem("tap2_done"), sem("tap1_done"), sem("tap0_done")
        silu_done, ff_done, u_hi_done, u_lo_done = sem("silu_done"), sem("ff_done"), sem("u_hi_done"), sem("u_lo_done")
        result_gained = sem("result_gained")
        result_scaled = {"dve": sem("result_scaled_dve"), "pool": sem("result_scaled_pool")}
        out_stored = [sem("out_stored0"), sem("out_stored1")]

        block = ctx.enter_context(nc.Block())

        def wait_output(eng, name, more=0):
            eng.wait_ge(out_ready, U[name] + 1 + more)

        def wait_evacuated(eng, name, laps=0):
            eng.wait_ge(evacuated[PLACE[name][0]], PLACE[name][1] + laps)

        def xm_lo(k):
            return xm_lo_parts[k // 4][:, k % 4]

        xn_lo_of = {"dve": [1, 3, 6], "pool": [0, 2, 4, 5, 7]}
        result_of = {"dve": [0, 1, 3, 4, 6, 7], "pool": [2, 5]}

        def psum(name):
            return pair[PLACE[name][0]]

        def freed(name):
            return evacuated[PLACE[name][0]]

        def logits_of(w, a):
            n = (w // PT_ + 1) * P
            return (("s", w, a), slice(0, n)) if wide(w) else (("s", w), slice(a * HALF, a * HALF + n))

        def transposed(name):
            w = name[1]
            nk = w // PT_ + 1
            if wide(w):
                return w, psum(name)[:, 0:nk * P].rearrange("p (k q) -> p k q", q=P), \
                    lambda buf: buf[:, w % 2, 0:nk, name[2]]
            both = psum(name)[:].rearrange("p (a k q) -> p a k q", a=2, q=P)
            return w, both[:, :, 0:nk], lambda buf: buf[:, w % 2, 0:nk].rearrange("p k a q -> p a k q")

        pt_number = {name: n + 1 for n, name in enumerate(x for w in range(PAIRS) for x in pt_names(w))}

        last_of = [("ikw")] + [("iq", p) for p in range(PT_)] + [("conv", n) for n in range(12)]
        for j in range(4):
            last_of += [("gc", 2 * j), ("gc", 2 * j + 1), ("co", 2 * j + 1)]
        last_of += [("q", p) for p in range(4)] + [("k", p) for p in range(4)] + [("v", p) for p in range(4)]
        last_of += [("ga", e) for e in range(8)] + [("ao", 2 * j + 1) for j in range(4)] + [("wo", e) for e in range(8)]
        last_of += [("up", 0, m) for m in range(4)]
        for g in range(1, FT // 2):
            last_of += [("up", g, m) for m in range(4)] + [("dn", g - 1, 3), ("dn", g - 1, 7)]
        last_of += [("dn", FT // 2 - 1, 3), ("dn", FT // 2 - 1, 7)]
        assert len(last_of) == N_CHUNKS

        @block.sync
        def _(sp):
            def load_chunk(c, lap=None):
                if c >= 3:
                    sp.wait_ge(w_lo_done, c - 2 + (0 if lap is None else 12 * lap))
                src = wts[c] if lap is None else wts[ds(c + 12 * lap, 1)].rearrange("a p n -> p (a n)")
                sp.dma_start(w_raw[:, c % 3].rearrange("p a b -> p (a b)"), src).then_inc(w_loaded[c % 3], 16)

            sp.dma_start(const[:], consts).then_inc(const_in, 16)
            for d in range(DT):
                if d < 2:
                    load_chunk(d)
                sp.dma_start(x_in[:, d], xT[d]).then_inc(x_loaded[d], 16)
            def move_queries(p):
                even, odd, low = iq_both[:, 2 * p].bitcast(f32), iq_both[:, 2 * p + 1].bitcast(f32), iq_lo[:, p % 2].bitcast(f32)
                sp.wait_ge(iq_hi_done, p + 1)
                sp.dma_start(odd[0:HD], even[HD:P]).then_inc(iq_moved[p][0], 16)
                sp.wait_ge(idx_lo_done, p + 2)
                sp.dma_start(odd[HD:P], low[HD:P]).then_inc(iq_moved[p][1], 16)
                sp.wait_ge(iq_moved[p][0], 16)
                sp.dma_start(even[HD:P], low[0:HD]).then_inc(iq_moved[p][2], 16)

            for c in range(2, C_AO + 5):
                load_chunk(c)
                if c in (6, 7, 8):
                    for p in {6: (0, 1), 7: (2,), 8: (3,)}[c]:
                        move_queries(p)
                j, at_end = divmod(c - (C_GROUP + 2 + 5), 3)
                if at_end == 0 and 0 <= j < 4:
                    for e in (2 * j, 2 * j + 1):
                        sp.wait_ge(bc_done, e + 1)
                        sp.dma_start(bc_dram[e], conv_c[:, 2 + e % 2]).then_inc(bc_stored[e % 2], 16)
                e = c - (C_GA + 5)
                if 0 <= e < DT:
                    wait_evacuated(sp, ("ga", e))
                    sp.dma_start(ga_dram[e], stage[:, e % 2]).then_inc(ga_stored[e % 2], 16)
            wait_evacuated(sp, s_names(PAIRS - 1)[-1])
            for n in range(2):
                sp.wait_ge(bc_stored[n], 16 * DT // 2)
                sp.wait_ge(ga_stored[n], 16 * DT // 2)
            for e in range(DT):
                if e >= 2:
                    sp.wait_ge(merged, e - 1)
                sp.dma_start(gate_in[:, e % 2, 0], ga_dram[e]).then_inc(gate_loaded[e % 2], 16)
                sp.dma_start(gate_in[:, e % 2, 1], bc_dram[e]).then_inc(gate_loaded[e % 2], 16)
                if e == 1:
                    sp.wait_ge(at_scaled, ST - 1 + PT_)
                    for d in range(DT):
                        sp.dma_start(h[:, d], xT[d]).then_inc(x_loaded[d], 16)
            for c in range(C_AO + 5, C_FF + 6):
                load_chunk(c)
            with sp.Fori(0, 5) as i:
                for n in range(12):
                    load_chunk(C_FF + 6 + n, i)
            for d in range(DT):
                who = "dve" if d in result_of["dve"] else "pool"
                sp.wait_ge(result_scaled[who], result_of[who].index(d) + 1)
                sp.dma_start(outT[d], result[:, d]).then_inc(out_stored[d % 2], 16)
            for n in range(2):
                sp.wait_ge(out_stored[n], 16 * DT // 2)

        @block.tensor
        def _(pe):
            def take_pair(name, more=0, laps=0):
                if PLACE[name][1] > 1:
                    pe.wait_ge(evacuated[PLACE[name][0]], PLACE[name][1] - 1 + laps)

            def three(out, w_h, w_l, x_h, x_l, first, last):
                nc.tensor.matmul(out, w_h, x_h, start=first, stop=False)
                nc.tensor.matmul(out, w_h, x_l, start=False, stop=False)
                return nc.tensor.matmul(out, w_l, x_h, start=False, stop=last)

            def product(name, slot, blocks, x_h, x_l, each_k=None, between=None, used=None):
                both = [slice(0, HALF), slice(HALF, S)]

                def step(n, b, cols):
                    return three(psum(name)[:, cols], w_hi[:, slot, b], w_lo[:, slot, b],
                                 x_h(n)[:, cols], x_l(n)[:, cols], n == 0, n == len(blocks) - 1)

                if between is None:
                    for cols in both:
                        for n, b in enumerate(blocks):
                            if each_k is not None and cols == both[0]:
                                each_k(n)
                            last = step(n, b, cols)
                else:
                    for n, b in enumerate(blocks):
                        between(n)
                        if each_k is not None:
                            each_k(n)
                        for cols in both:
                            last = step(n, b, cols)
                        if used is not None and n < len(blocks) - 1:
                            last.then_inc(used, 1)
                last.then_inc(out_ready, 1)

            def chunk(c, names, x_h, x_l, each_k=None, lap=None, laps_psum=0, between=None, used=None):
                pe.wait_ge(w_lo_done, c + 1 + (0 if lap is None else 12 * lap))
                per = 8 // len(names)
                for n, name in enumerate(names):
                    take_pair(name, laps=laps_psum)
                    product(name, c % 2, range(n * per, (n + 1) * per), x_h, x_l, each_k, between, used)

            def norm_sum(n):
                name = f"n{n}_sum"
                take_pair(name)
                if n == 0:
                    pe.wait_ge(fixed_ready, 3)
                pe.wait_ge(acc_done, DT * (n + 1))
                for t in range(ST):
                    last = nc.tensor.matmul(psum(name)[:, t:t + 1], nrm_acc[:, t * P:(t + 1) * P], ones[:, 0:1],
                                            start=True, stop=True)
                last.then_inc(out_ready, 1)

            def norm_spread(n):
                name = f"n{n}_bc"
                take_pair(name)
                pe.wait_ge(wide_done, n + 1)
                for t in range(ST):
                    last = nc.tensor.transpose(psum(name)[:, t * P:(t + 1) * P], nrm_wide[min(n, 1)][:, t], ident[:])
                last.then_inc(out_ready, 1)

            def from_xn():
                return (lambda k: xn_hi[:, k]), (lambda k: xn_lo[:, k])

            def first_two(n, k):
                name = ("ikw", ("iq", 0))[n]
                if k == 0:
                    pe.wait_ge(w_lo_done, n + 1)
                for half in range(2):
                    cols = slice(half * HALF, (half + 1) * HALF)
                    last = three(psum(name)[:, cols], w_hi[:, n, k], w_lo[:, n, k],
                                 xn_hi[:, k, cols], xn_lo[:, k, cols], k == 0, k == DT - 1)
                if k == DT - 1:
                    last.then_inc(out_ready, 1)

            for k in range(DT):
                pe.wait_ge(gained_lo, k + 1)
                first_two(0, k)
                if k:
                    first_two(1, k - 1)
            first_two(1, DT - 1)
            norm_sum(0)

            def xn_ready(k):
                who = "dve" if k in xn_lo_of["dve"] else "pool"
                pe.wait_ge(xn_lo_done[who], xn_lo_of[who].index(k) + 1)

            chunk(C_IQ + 1, [("iq", 1)], *from_xn(), between=lambda n: norm_spread(0) if n == 5 else None)
            chunk(C_IQ + 2, [("iq", 2)], *from_xn())
            take_pair("iw_tok")
            pe.wait_ge(idx_scaled, 1)
            for t in range(ST):
                last = nc.tensor.transpose(psum("iw_tok")[:, t * NH:(t + 1) * NH],
                                           stage[HD:HD + NH, 0, t * P:(t + 1) * P], ident[HD:HD + NH, HD:HD + NH])
            last.then_inc(out_ready, 1)
            chunk(C_IQ + 3, [("iq", 3)], *from_xn(), between=lambda k: None, used=gained_used)
            for s in ik_copied:
                pe.wait_ge(s, 16)
            def dots(t, hh):
                name = ("dots", t, hh)
                p = hh // 2
                take_pair(name)
                for s in iq_moved[p]:
                    pe.wait_ge(s, 16)
                for k0 in range(0, (t + 1) * P, HALF):
                    cols = slice(k0, min(k0 + HALF, (t + 1) * P))
                    q = iq_both[:, hh, t * P:(t + 1) * P]
                    nc.tensor.matmul(psum(name)[:, cols], q, ik_hi[:, cols], start=True, stop=False)
                    last = nc.tensor.matmul(psum(name)[:, cols], q, ik_lo[:, cols], start=False, stop=True)
                last.then_inc(out_ready, 1)

            for n in range(3 * CT):
                def between(k):
                    for d in dots_before(n, k):
                        dots(*d)

                chunk(C_CONV + n, [("conv", n)], *from_xn(),
                      each_k=xn_ready if n == 0 else None, between=between if n < MIXED else None)
            for j in range(4):
                chunk(C_GROUP + 3 * j, [("gc", 2 * j)], *from_xn())
                chunk(C_GROUP + 3 * j + 1, [("gc", 2 * j + 1)], *from_xn())
                chunk(C_GROUP + 3 * j + 2, [("co", 2 * j), ("co", 2 * j + 1)],
                      lambda k: cv_hi[:, k], lambda k: cv_lo[:, k],
                      each_k=(lambda k: pe.wait_ge(conv_lo_done, k + 1)) if j == 0 else None)
            for p in range(PT_):
                chunk(C_Q + p, [("q", p)], *from_xn())
            for p in range(PT_):
                chunk(C_K + p, [("k", p)], *from_xn())

            def v_transposes(p):
                take_pair(("vt", p))
                wait_evacuated(pe, ("v", p))
                for t in range(ST):
                    last = nc.tensor.transpose(psum(("vt", p))[:, t * P:(t + 1) * P],
                                               stage[:, 0, t * P:(t + 1) * P], ident[:])
                last.then_inc(out_ready, 1)

            for p in range(PT_):
                chunk(C_V + p, [("v", p)], *from_xn())
                if p:
                    v_transposes(p - 1)
            chunk(C_GA, [("ga", 0)], *from_xn())
            v_transposes(PT_ - 1)
            for e in range(1, DT):
                chunk(C_GA + e, [("ga", e)], *from_xn())

            def logits(w, a):
                t, p = divmod(w, PT_)
                r = slice(HD * a, HD * a + HD)
                name, c = logits_of(w, a)
                if a == 0:
                    pe.wait_ge(qs_lo_done, t + 1)
                if wide(w) or a == 0:
                    take_pair(name)
                for k0 in range(0, (t + 1) * P, HALF):
                    k1 = min(k0 + HALF, (t + 1) * P)
                    last = three(psum(name)[:, c.start + k0:c.start + k1],
                                 qs_hi[r, t % 2, p], qs_lo[r, t % 2, p],
                                 k_hi[r, p, k0:k1], k_lo[r, p, k0:k1], True, True)
                if wide(w) or a == 1:
                    last.then_inc(out_ready, 1)

            def transpose_probs(w, a):
                name = pt_names(w)[a if wide(w) else 0]
                c0 = 0 if wide(w) else a * HALF
                if wide(w) or a == 0:
                    take_pair(name)
                pe.wait_ge(exp_done, 2 * w + a + 1)
                for kb in range(w // PT_ + 1):
                    last = nc.tensor.transpose(psum(name)[:, c0 + kb * P:c0 + (kb + 1) * P],
                                               probs[:, w % 2, a, kb * P:(kb + 1) * P], ident[:])
                if wide(w) or a == 1:
                    last.then_inc(out_ready, 1)

            def probs_times_v(w):
                t, p = divmod(w, PT_)
                take_pair(("o", w))
                for name in pt_names(w):
                    wait_evacuated(pe, name)
                for kb in range(t + 1):
                    last = three(psum(("o", w))[:, 0:2 * P], v_hi[:, kb, p * P:(p + 1) * P],
                                 v_lo[:, kb, p * P:(p + 1) * P],
                                 pt_hi[:, w % 2, kb].rearrange("p a q -> p (a q)"),
                                 pt_lo[:, w % 2, kb].rearrange("p a q -> p (a q)"), kb == 0, kb == t)
                last.then_inc(out_ready, 1)

            def reciprocals(t):
                name = ("sums", t)
                take_pair(name)
                pe.wait_ge(rc_widened, t + 1)
                for p in range(PT_):
                    last = nc.tensor.transpose(psum(name)[:, p * P:(p + 1) * P], rc_wide[:, t % 2, p], ident[:])
                last.then_inc(out_ready, 1)

            pe.wait_ge(k_lo_done, PT_)
            pe.wait_ge(v_lo_done, PT_)
            for w in range(2):
                for a in range(2):
                    logits(w, a)
            for w in range(PAIRS + 1):
                if w < PAIRS and wide(w):
                    for a in range(2):
                        transpose_probs(w, a)
                        if w + 2 < PAIRS:
                            logits(w + 2, a)
                elif w < PAIRS:
                    for a in range(2):
                        transpose_probs(w, a)
                    for a in range(2):
                        logits(w + 2, a)
                if w >= 1:
                    probs_times_v(w - 1)
                if w >= 1 and w % PT_ == 0 and w < PAIRS:
                    reciprocals(w // PT_ - 1)
                if w == PAIRS - 1:
                    reciprocals(ST - 1)

            for j in range(4):
                chunk(C_AO + j, [("ao", 2 * j), ("ao", 2 * j + 1)], lambda k: at_hi[:, k], lambda k: at_lo[:, k],
                      each_k=(lambda k: pe.wait_ge(at_lo_done, k + 1)) if j == 0 else None)
            for e in range(DT):
                chunk(C_WO + e, [("wo", e)], lambda k: mg_hi[:, k], lambda k: mg_lo[:, k],
                      each_k=(lambda k: pe.wait_ge(mg_lo_done, k + 1)) if e == 0 else None)

            def up(g, m, c, more=None, laps=0):
                chunk(c + m, [("up", g, m)], lambda k: xm_hi[:, k], xm_lo,
                      each_k=(lambda k: pe.wait_ge(gained_lo, DT + k + 1)) if g == 0 and m == 0 else None,
                      lap=more, laps_psum=laps)

            def down(g, c, more=None, laps=0):
                pe.wait_ge(u_lo_done, 2 * g + 2 + (0 if more is None else 4 * more))
                for n in range(2):
                    chunk(c + n, [("dn", g, 4 * n + e) for e in range(4)],
                          lambda k: u_hi[:, (g + 1) % 2, k], lambda k: u_lo[:, (g + 1) % 2, k], lap=more, laps_psum=laps)

            up(0, 0, C_FF)
            norm_sum(1)
            up(0, 1, C_FF)
            norm_spread(1)
            up(0, 2, C_FF)
            up(0, 3, C_FF)
            with pe.Fori(0, 5) as i:
                for n in range(2):
                    for m in range(4):
                        up(1 + n, m, C_FF + 4 + 6 * n, i, 6 * i)
                    down(n, C_FF + 8 + 6 * n, i, 6 * i)
            down(FT // 2 - 1, N_CHUNKS - 2)
            norm_sum(2)
            norm_spread(2)

        @block.scalar
        def _(act):
            A = nc.scalar

            def split(c, lap=None):
                act.wait_ge(w_loaded[c % 3], 16 * (c // 3 + 1) + (0 if lap is None else 64 * lap))
                if c >= 2:
                    wait_output(act, last_of[c - 2], 0 if lap is None else 24 * lap)
                A.copy(w_hi[:, c % 2], w_raw[:, c % 3]).then_inc(w_hi_done, 1)

            def square(n, d, src):
                if DT * n + d >= 2:
                    act.wait_ge(acc_done, DT * n + d - 1)
                A.activation(stage[:, d % 2], src[:, d], ACT.Square).then_inc(square_done, 1)

            def gained(d, src, g0, hi):
                A.activation(hi[:, d], src[:, d], ACT.Copy, scale=const[:, g0 + d:g0 + d + 1]).then_inc(gained_hi, 1)

            def sqrt(n):
                act.wait_ge(var_done, n + 1)
                A.activation(small[:, 8:16], small[:, 0:8], ACT.Sqrt).then_inc(sqrt_done, 1)

            def spread(n):
                wait_output(act, f"n{n}_bc")
                A.copy(rrms[min(n, 1)][:], psum(f"n{n}_bc")[:]).then_inc(freed(f"n{n}_bc"), 1)

            def after(c):
                split(c + 2)

            split(0)
            act.wait_ge(const_in, 16)
            for d in range(DT):
                act.wait_ge(x_loaded[d], 16)
                gained(d, x_in, T_GMIX, xn_hi)
                square(0, d, x_in)
                if d == 0:
                    split(1)
            after(C_IKW)
            act.wait_ge(acc_done, DT)
            A.copy(stage[0:HD + NH, 0], psum("ikw")[0:HD + NH]).then_inc(freed("ikw"), 1)
            wait_output(act, ("iq", 0))
            A.copy(stage[:, 1], psum(("iq", 0))[:]).then_inc(freed(("iq", 0)), 1)
            after(C_IQ)
            sqrt(0)
            spread(0)
            after(C_IQ + 1)
            act.wait_ge(idx_scaled, 1)
            A.copy(ik_hi[0:HD], stage[0:HD, 0]).then_inc(ik_hi_done, 1)
            act.wait_ge(idx_scaled, 2)
            A.copy(iq_both[:, 0], stage[:, 1]).then_inc(iq_hi_done, 1)
            act.wait_ge(ik_hi_done, 1)
            act.dma_start(ik_hi[HD:P].bitcast(f32), ik_hi[0:HD].bitcast(f32)).then_inc(ik_copied[0], 16)
            act.wait_ge(idx_lo_done, 1)
            act.dma_start(ik_lo[HD:P].bitcast(f32), ik_lo[0:HD].bitcast(f32)).then_inc(ik_copied[1], 16)
            for p in range(1, PT_):
                if p == PT_ - 1:
                    for d in range(DT):
                        act.wait_ge(x_scaled, d + 1)
                        if d < DT - 1:
                            act.wait_ge(gained_used, d + 1)
                        else:
                            wait_output(act, ("iq", p))
                        A.copy(xn_hi[:, d], x_in[:, d]).then_inc(xn_hi_done, 1)
                if p == 2:
                    after(C_IQ + p)
                wait_evacuated(act, ("iq", p))
                A.copy(iq_both[:, 2 * p], iq_raw[:, p % 2]).then_inc(iq_hi_done, 1)
            def relu(t, hh):
                name, n, number = ("dots", t, hh), (t + 1) * P, NH * (t - 2) + hh
                wait_output(act, name)
                if number >= 2:
                    act.wait_ge(score_step, number - 1)
                A.activation(rel[:, hh % 2, 0:n], psum(name)[:, 0:n], ACT.Relu).then_inc(freed(name), 1)

            after(C_IQ + PT_ - 1)

            def conv_hi(p):
                act.wait_ge(conv_step, 5 * (p + 1))
                A.copy(cv_hi[:, p], conv_b[:, p]).then_inc(conv_hi_done, 1)

            for n in range(3 * CT):
                p, which = divmod(n, 3)
                for d in dots_before(n):
                    relu(*d)
                wait_output(act, ("conv", n))
                A.copy((conv_h, conv_c, conv_b)[which][:, p], psum(("conv", n))[:]).then_inc(freed(("conv", n)), 1)
                after(C_CONV + n)
                if n in (8, 11):
                    conv_hi((n - 8) // 3)
            for j in range(4):
                for n in range(2):
                    e = 2 * j + n
                    wait_output(act, ("gc", e))
                    if e < 2:
                        act.wait_ge(conv_step, 5 * e + 4)
                    if e >= 2:
                        act.wait_ge(bc_done, e - 1)
                    A.activation(conv_c[:, n], psum(("gc", e))[:], ACT.Sigmoid,
                                 bias=const[:, T_BIAS + DT + e:T_BIAS + DT + e + 1]).then_inc(freed(("gc", e)), 1)
                    after(C_GROUP + 3 * j + n)
                    if j == 0 and n == 0:
                        conv_hi(2)
                        conv_hi(3)
                for n in range(2):
                    e = 2 * j + n
                    wait_output(act, ("co", e))
                    if e >= 2:
                        act.wait_ge(bc_stored[e % 2], 16 * (e // 2))
                    A.copy(conv_c[:, 2 + n], psum(("co", e))[:]).then_inc(freed(("co", e)), 1)
                after(C_GROUP + 3 * j + 2)
            for p in range(PT_):
                wait_output(act, ("q", p))
                if p == 0:
                    for n in range(2):
                        act.wait_ge(bc_stored[n], 16 * DT // 2)
                A.copy(q_raw[:, p], psum(("q", p))[:]).then_inc(freed(("q", p)), 1)
                after(C_Q + p)
            for p in range(PT_):
                wait_output(act, ("k", p))
                if p >= 2:
                    act.wait_ge(k_lo_done, p - 1)
                A.copy(stage[:, p % 2], psum(("k", p))[:]).then_inc(k_staged, 1)
                A.copy(k_hi[:, p], psum(("k", p))[:]).then_inc(freed(("k", p)), 1)
                after(C_K + p)

            def v_split(p):
                wait_output(act, ("vt", p))
                src = psum(("vt", p))[:].rearrange("p (t c) -> p t c", c=P)
                if p:
                    act.wait_ge(v_lo_done, p)
                A.copy(stage[:, 1], psum(("vt", p))[:]).then_inc(v_staged, 1)
                A.copy(v_hi[:, :, p * P:(p + 1) * P], src).then_inc(freed(("vt", p)), 1)

            for p in range(PT_):
                wait_output(act, ("v", p))
                if p == 0:
                    act.wait_ge(k_lo_done, PT_)
                else:
                    wait_output(act, ("vt", p - 1))
                A.copy(stage[:, 0], psum(("v", p))[:]).then_inc(freed(("v", p)), 1)
                after(C_V + p)
                if p:
                    v_split(p - 1)
            for e in range(DT):
                if e == 1:
                    v_split(PT_ - 1)
                    act.wait_ge(v_lo_done, PT_)
                wait_output(act, ("ga", e))
                if e == 0:
                    wait_output(act, ("vt", PT_ - 1))
                if e >= 2:
                    act.wait_ge(ga_stored[e % 2], 16 * (e // 2))
                A.activation(stage[:, e % 2], psum(("ga", e))[:], ACT.Sigmoid,
                             bias=const[:, T_BIAS + e:T_BIAS + e + 1]).then_inc(freed(("ga", e)), 1)
                after(C_GA + e)

            def q_split(t):
                if t == 0:
                    wait_output(act, ("ga", DT - 1))
                else:
                    wait_output(act, s_names(PT_ * (t - 1))[-1])
                A.copy(qs_hi[:, t % 2], q_raw[:, :, t * P:(t + 1) * P]).then_inc(qs_hi_done, 1)

            def exponentials(w, a):
                t, p = divmod(w, PT_)
                x = probs[:, w % 2, a, 0:(t + 1) * P]
                if wide(w) or a == 1:
                    wait_evacuated(act, logits_of(w, a)[0])
                else:
                    act.wait_ge(first_max_done, w + 1)
                if t >= 2 and p == 0 and a == 0:
                    act.wait_ge(recip_done, t - 1)
                k, c = 2 * (w % 2) + a, 2 * p + a
                A.activation(x, x, ACT.Exp, scale=-1.0, bias=negmax[:, k:k + 1],
                             accum_out=sums[:, t % 2, c:c + 1]).then_inc(exp_done, 1)

            def probs_hi(name):
                w, src, place = transposed(name)
                wait_output(act, name)
                if w >= 2:
                    wait_output(act, ("o", w - 2))
                A.copy(place(pt_hi), src).then_inc(pt_hi_done, 1)

            def outputs(w):
                t, p = divmod(w, PT_)
                name = ("o", w)
                wait_output(act, name)
                cols = slice(t * P, (t + 1) * P)
                A.copy(q_raw[0:HD, p, cols], psum(name)[0:HD, 0:P])
                A.copy(q_raw[HD:P, p, cols], psum(name)[HD:P, P:2 * P]).then_inc(freed(name), 1)

            def reciprocals(t):
                wait_output(act, ("sums", t))
                if t >= 2:
                    act.wait_ge(at_scaled, t - 1)
                A.copy(rc_tok[:, t % 2].rearrange("p a b -> p (a b)"),
                       psum(("sums", t))[:, 0:PT_ * P]).then_inc(freed(("sums", t)), 1)

            def attention_hi(p):
                act.wait_ge(at_scaled, ST + p)
                A.copy(at_hi[:, p], q_raw[:, p]).then_inc(at_hi_done, 1)

            q_split(0)
            exponentials(0, 0)
            exponentials(0, 1)
            for w in range(PAIRS + 2):
                if w >= 2:
                    outputs(w - 2)
                if w == PAIRS:
                    reciprocals(ST - 1)
                    attention_hi(0)
                    attention_hi(1)
                if PT_ <= w < PAIRS and w % PT_ == 1:
                    reciprocals(w // PT_ - 1)
                names = pt_names(w) if w < PAIRS else []
                for n in range(2):
                    if n < len(names):
                        probs_hi(names[n])
                    if w + 1 < PAIRS:
                        exponentials(w + 1, n)
                if w % PT_ == 0 and w // PT_ + 1 < ST:
                    q_split(w // PT_ + 1)
            attention_hi(2)
            attention_hi(3)

            for e in range(DT):
                act.wait_ge(merged, e + 1)
                A.copy(mg_hi[:, e], stage[:, e % 2]).then_inc(mg_hi_done, 1)
                if e % 2:
                    after(C_AO + e // 2)

            def h_ready(e):
                wait_evacuated(act, ("wo", e))
                if e == 0:
                    act.wait_ge(mg_lo_done, DT)
            for d in range(DT):
                after_c = C_WO + d
                wait_output(act, ("wo", d))
                split(after_c + 2)
                h_ready(d)
                gained(d, h, T_GFFN, xm_hi)
                square(1, d, h)

            def tap2(g, m, col, laps=0):
                if g == 0 and m == 0:
                    act.wait_ge(first_up_scaled, 1)
                else:
                    wait_evacuated(act, ("up", g, m), laps)
                A.activation(ff_t[:, m], up_out[:, m % 2], ACT.Copy, scale=const[:, col]).then_inc(tap2_done, 1)

            def ffn_group(g, c, first=False, i=None):
                j = 0 if i is None else i
                lap = i
                groups = g + 2 * j
                for m in range(4):
                    if not first and m in (1, 3):
                        act.wait_ge(u_lo_done, 2 * groups - 1 + m // 2)
                    if not first and m in (0, 2):
                        act.wait_ge(silu_done, 2 * groups - 1 + m // 2)
                    col = T_FCONV + 12 * g + 3 * m + 2
                    col = slice(col, col + 1) if i is None else ds(col + 24 * i, 1)
                    wait_output(act, ("up", g, m), 24 * j)
                    if first and m == 0:
                        A.copy(up_out[:, 0], psum(("up", 0, 0))[:]).then_inc(freed(("up", 0, 0)), 1)
                        split(c + 2)
                        sqrt(1)
                        wait_output(act, ("up", 0, 1))
                        split(c + 3)
                        spread(1)
                    elif not (first and m == 1):
                        split(c + m + 2, lap)
                    tap2(g, m, col, 6 * j)
                    if m in (1, 3):
                        if not first:
                            act.wait_ge(ff_done, 2 * groups - 1 + m // 2)
                        act.wait_ge(tap0_done, 4 * groups + m)
                        A.activation(stage[:, m // 2], ff_t[:, m - 1], ACT.Silu).then_inc(silu_done, 1)
                    if m == 2:
                        ffn_hi(g, 0, groups, j)

            def ffn_hi(g, a, groups, j):
                act.wait_ge(ff_done, 2 * groups + a + 1)
                A.copy(u_hi[:, (g + 1) % 2, a], ff_t[:, 2 * a + 1]).then_inc(u_hi_done, 1)

            ffn_group(0, C_FF, first=True)
            ffn_hi(0, 1, 0, 0)
            with act.Fori(0, 5) as i:
                for n in range(2):
                    g = 1 + n
                    ffn_group(g, C_FF + 4 + 6 * n, i=i)
                    ffn_hi(g, 1, g + 2 * i, i)
                    for k in range(2):
                        wait_output(act, ("dn", n, 4 * k + 3), 24 * i)
                        c = C_FF + 8 + 6 * n + k
                        split(c + 2, i)
            for d in range(DT):
                wait_evacuated(act, ("dn", FT // 2 - 1, d))
                square(2, d, h)
                A.activation(result[:, d], h[:, d], ACT.Copy,
                             scale=const[:, T_GFIN + d:T_GFIN + d + 1]).then_inc(result_gained, 1)
            sqrt(2)
            spread(2)

        @block.gpsimd
        def _(pool):
            G_ = nc.gpsimd

            def lo(c, lap=None):
                pool.wait_ge(w_hi_done, c + 1 + (0 if lap is None else 12 * lap))
                G_.tensor_tensor(w_lo[:, c % 2], w_raw[:, c % 3], w_hi[:, c % 2].bitcast(f32),
                                 ALU.subtract).then_inc(w_lo_done, 1)

            G_.memset(ident[:], 0.0).then_inc(ident_zero, 1)
            G_.memset(ones[:], 1.0).then_inc(fixed_ready, 1)
            G_.memset(mask[:, 0:mask_at(2)], 0.0).then_inc(ident_zero, 1)
            pool.wait_ge(ident_zero, 2)
            G_.affine_select(out=ident[:], in_=ident[:], compare_op=ALU.not_equal, fill=1.0, base=0,
                             pattern=[[-1, P]], channel_multiplier=1).then_inc(fixed_ready, 1)
            for t in range(2):
                diag = mask[:, mask_at(t) + t * P:mask_at(t + 1)]
                last = G_.affine_select(out=diag, in_=diag, compare_op=ALU.is_ge, fill=MASKED, base=0,
                                        pattern=[[-1, P]], channel_multiplier=1)
            last.then_inc(fixed_ready, 1)
            for c in range(C_CONV + 1):
                lo(c)
            for d in xn_lo_of["pool"]:
                pool.wait_ge(xn_hi_done, d + 1)
                G_.tensor_tensor(xn_lo[:, d], x_in[:, d], xn_hi[:, d].bitcast(f32),
                                 ALU.subtract).then_inc(xn_lo_done["pool"], 1)

            def causal(t):
                pool.wait_ge(score_step, NH * (t - 1))
                diag = mask[:, mask_at(t) + t * P:mask_at(t + 1)]
                G_.affine_select(out=diag, in_=diag, compare_op=ALU.is_ge, fill=ACAUSAL, base=0,
                                 pattern=[[-1, P]], channel_multiplier=1).then_inc(causal_done, 1)

            for c in range(C_CONV + 1, C_GROUP + 4):
                lo(c)
                if C_CONV + 2 <= c < C_CONV + ST:
                    causal(c - C_CONV)
                if c in (C_CONV + 10, C_CONV + 13, C_GROUP + 2):
                    for p in {C_CONV + 10: (0,), C_CONV + 13: (1,), C_GROUP + 2: (2, 3)}[c]:
                        pool.wait_ge(conv_hi_done, p + 1)
                        G_.tensor_tensor(cv_lo[:, p], conv_b[:, p], cv_hi[:, p].bitcast(f32),
                                         ALU.subtract).then_inc(conv_lo_done, 1)
            for j in range(4):
                lo(C_GROUP + 3 * j + 4)
                for n in range(2):
                    e = 2 * j + n
                    wait_evacuated(pool, ("gc", e))
                    wait_evacuated(pool, ("co", e))
                    G_.tensor_tensor(conv_c[:, 2 + n], conv_c[:, 2 + n], conv_c[:, n],
                                     ALU.mult).then_inc(bc_done, 1)
                if j < 3:
                    lo(C_GROUP + 3 * j + 5)
                    lo(C_GROUP + 3 * j + 6)
            for c in range(C_GROUP + 14, C_K + 2):
                lo(c)
            for p in range(PT_):
                lo(C_K + p + 2)
                pool.wait_ge(k_staged, p + 1)
                wait_evacuated(pool, ("k", p))
                G_.tensor_tensor(k_lo[:, p], stage[:, p % 2], k_hi[:, p].bitcast(f32),
                                 ALU.subtract).then_inc(k_lo_done, 1)

            def v_lo_part(p):
                pool.wait_ge(v_staged, p + 1)
                wait_evacuated(pool, ("vt", p))
                G_.tensor_tensor(v_lo[:, :, p * P:(p + 1) * P],
                                 stage[:, 1].rearrange("p (t c) -> p t c", c=P),
                                 v_hi[:, :, p * P:(p + 1) * P].bitcast(f32), ALU.subtract).then_inc(v_lo_done, 1)

            for p in range(PT_):
                lo(C_V + p + 2)
                if p:
                    v_lo_part(p - 1)
            lo(C_GA + 2)
            v_lo_part(PT_ - 1)
            for c in range(C_GA + 3, C_AO + 2):
                lo(c)
            def widen(t):
                pool.wait_ge(recip_done, t + 1)
                if t >= 2:
                    wait_output(pool, ("sums", t - 2))
                G_.tensor_copy(rc_wide[:, t % 2].rearrange("p a (b c) -> p (a b) c", c=HD),
                               recips[:, t % 2].unsqueeze(2).to_broadcast([P, NH, HD])).then_inc(rc_widened, 1)

            def scale_outputs(t, pairs=slice(0, PT_)):
                wait_evacuated(pool, ("sums", t))
                for p in range(pairs.start, pairs.stop):
                    wait_evacuated(pool, ("o", PT_ * t + p))
                x = q_raw[:, pairs, t * P:(t + 1) * P]
                G_.tensor_tensor(x, x, rc_tok[:, t % 2, pairs], ALU.mult).then_inc(at_scaled, 1)

            for t in range(ST):
                widen(t)
                if t:
                    scale_outputs(t - 1)
            for p in range(PT_):
                scale_outputs(ST - 1, slice(p, p + 1))
            for c in range(C_AO + 2, C_FF + 6):
                lo(c)

            def u_lo_part(g, a, n):
                pool.wait_ge(u_hi_done, n)
                G_.tensor_tensor(u_lo[:, (g + 1) % 2, a], ff_t[:, 2 * a + 1], u_hi[:, (g + 1) % 2, a].bitcast(f32),
                                 ALU.subtract).then_inc(u_lo_done, 1)

            u_lo_part(0, 0, 1)
            u_lo_part(0, 1, 2)
            with pool.Fori(0, 5) as i:
                for n in range(2):
                    g = 1 + n
                    for m in range(6):
                        lo(C_FF + 6 + 6 * n + m, i)
                        if m == 2:
                            u_lo_part(g, 0, 4 * i + 2 * g + 1)
                        if m == 3:
                            u_lo_part(g, 1, 4 * i + 2 * g + 2)
            for n, d in enumerate(result_of["pool"]):
                pool.wait_ge(result_gained, d + 1)
                wait_evacuated(pool, "n2_bc")
                G_.tensor_tensor(result[:, d], result[:, d], rrms[1][:], ALU.mult).then_inc(result_scaled["pool"], 1)

        @block.vector
        def _(dve):
            V = nc.vector

            steps = {}

            def step(s, ins):
                steps[s.name] = steps.get(s.name, 0) + 1
                ins.then_inc(s, 1)
                dve.wait_ge(s, steps[s.name])

            def accumulate(n, d):
                dve.wait_ge(square_done, DT * n + d + 1)
                if DT * n + d:
                    dve.wait_ge(acc_done, DT * n + d)
                if d == 0:
                    if n:
                        wait_output(dve, f"n{n - 1}_sum")
                    V.tensor_copy(nrm_acc[:], stage[:, 0]).then_inc(acc_done, 1)
                else:
                    V.tensor_tensor(nrm_acc[:], nrm_acc[:], stage[:, d % 2], ALU.add).then_inc(acc_done, 1)

            def norm_rms(n):
                v, s, y, t = small[:, 0:8], small[:, 8:16], small[:, 16:24], small[:, 24:32]
                a = f"n{n}_sum"
                wait_output(dve, a)
                if n:
                    dve.wait_ge(wide_done, n)
                V.tensor_scalar(v, psum(a)[:, 0:ST], 1.0 / D, EPS, ALU.mult, ALU.add).then_inc(freed(a), 1)
                wait_evacuated(dve, a)
                V.tensor_copy(t, v).then_inc(var_done, 1)
                dve.wait_ge(sqrt_done, n + 1)
                step(newton, V.reciprocal(y, s))
                step(newton, V.tensor_tensor(t, y, y, ALU.mult))
                step(newton, V.tensor_tensor(t, t, v, ALU.mult))
                step(newton, V.tensor_scalar(t, t, -0.5, 1.5, ALU.mult, ALU.add))
                step(newton, V.tensor_tensor(y, y, t, ALU.mult))
                if n == 0:
                    dve.wait_ge(fixed_ready, 3)
                else:
                    wait_output(dve, f"n{n - 1}_bc")
                V.tensor_copy(nrm_wide[min(n, 1)][:], y.unsqueeze(2).to_broadcast([P, ST, P])).then_inc(wide_done, 1)

            def gained_low(n, d, src, g0, lo_part, hi):
                dve.wait_ge(gained_hi, DT * n + d + 1)
                V.scalar_tensor_tensor(lo_part, src[:, d], const[:, g0 + d:g0 + d + 1], hi[:, d].bitcast(f32),
                                       ALU.mult, ALU.subtract).then_inc(gained_lo, 1)

            dve.wait_ge(const_in, 16)
            for d in range(DT):
                gained_low(0, d, x_in, T_GMIX, xn_lo[:, d], xn_hi)
                accumulate(0, d)
            norm_rms(0)
            wait_evacuated(dve, "n0_bc")
            wait_evacuated(dve, "ikw")
            x = stage[0:HD + NH, 0]
            V.tensor_tensor(x, x, rrms[0][0:HD + NH], ALU.mult).then_inc(idx_scaled, 1)
            wait_evacuated(dve, ("iq", 0))
            V.tensor_tensor(stage[:, 1], stage[:, 1], rrms[0][:], ALU.mult).then_inc(idx_scaled, 1)

            def scale_iq(p):
                wait_output(dve, ("iq", p))
                if p == 3:
                    dve.wait_ge(idx_lo_done, 3)
                V.tensor_tensor(iq_raw[:, p % 2], psum(("iq", p))[:], rrms[0][:], ALU.mult).then_inc(freed(("iq", p)), 1)

            def iq_low(p):
                dve.wait_ge(iq_hi_done, p + 1)
                if p:
                    wait_evacuated(dve, ("iq", p))
                else:
                    dve.wait_ge(idx_scaled, 2)
                if p >= 2:
                    for s in iq_moved[p - 2][1:]:
                        dve.wait_ge(s, 16)
                hi = iq_both[:, 2 * p].bitcast(f32)
                V.tensor_tensor(iq_lo[:, p % 2], iq_raw[:, p % 2] if p else stage[:, 1], hi,
                                ALU.subtract).then_inc(idx_lo_done, 1)

            def scale_x(d):
                V.scalar_tensor_tensor(x_in[:, d], x_in[:, d], const[:, T_GMIX + d:T_GMIX + d + 1], rrms[0][:],
                                       ALU.mult, ALU.mult).then_inc(x_scaled, 1)

            scale_iq(1)
            dve.wait_ge(ik_hi_done, 1)
            V.tensor_tensor(ik_lo[0:HD], stage[0:HD, 0], ik_hi[0:HD].bitcast(f32),
                            ALU.subtract).then_inc(idx_lo_done, 1)
            dve.wait_ge(gained_lo, DT)
            iq_low(0)
            iq_low(1)
            for d in range(4):
                scale_x(d)
            scale_iq(2)
            iq_low(2)

            def xn_low(d):
                dve.wait_ge(xn_hi_done, d + 1)
                V.tensor_tensor(xn_lo[:, d], x_in[:, d], xn_hi[:, d].bitcast(f32),
                                ALU.subtract).then_inc(xn_lo_done["dve"], 1)

            for d in range(4, DT):
                scale_x(d)
                if d in (5, 7):
                    xn_low(xn_lo_of["dve"][d // 2 - 2])
            xn_low(xn_lo_of["dve"][2])
            wait_output(dve, "iw_tok")
            V.tensor_scalar(iw_tok[:].rearrange("p t h -> p (t h)"), psum("iw_tok")[:, 0:ST * NH], iw_scale, None,
                            ALU.mult).then_inc(freed("iw_tok"), 1)
            scale_iq(3)
            iq_low(3)
            wait_evacuated(dve, "iw_tok")
            def add_score(t, hh):
                score = mask[:, mask_at(t):mask_at(t + 1)]
                wait_evacuated(dve, ("dots", t, hh))
                r = rel[:, hh % 2, 0:(t + 1) * P]
                w = iw_tok[:, t, hh:hh + 1]
                if hh == 0:
                    step(score_step, V.tensor_scalar(score, r, w, None, ALU.mult))
                else:
                    step(score_step, V.scalar_tensor_tensor(score, r, w, score, ALU.mult, ALU.add))

            done_rounds = [0]

            def topk_rounds(t, rounds):
                score = mask[:, mask_at(t):mask_at(t + 1)]
                first = 2 * done_rounds[0]
                dve.wait_ge(causal_done, t - 1)
                for r in range(rounds):
                    if first or r:
                        dve.wait_ge(topk_step, first + 2 * r)
                    V.max(top8[:], score).then_inc(topk_step, 1)
                    dve.wait_ge(topk_step, first + 2 * r + 1)
                    V.match_replace(score, top8[:], score, TAKEN).then_inc(topk_step, 1)
                done_rounds[0] += rounds
                dve.wait_ge(topk_step, 2 * done_rounds[0])

            def choose(t):
                score = mask[:, mask_at(t):mask_at(t + 1)]
                V.tensor_scalar(score, score, UNCHOSEN, MASKED, ALU.is_gt, ALU.mult).then_inc(mask_done, 1)

            def convolve(p):
                for n in range(3):
                    wait_evacuated(dve, ("conv", 3 * p + n))

                def tap(k):
                    return const[:, T_CONV + k * CT + p:T_CONV + k * CT + p + 1]

                u, y, b = conv_c[:, p], conv_h[:, p], conv_b[:, p]
                step(conv_step, V.tensor_tensor(u, u, y, ALU.mult))
                step(conv_step, V.tensor_scalar(y, u, tap(2), None, ALU.mult))
                step(conv_step, V.scalar_tensor_tensor(y[:, 1:S], u[:, 0:S - 1], tap(1), y[:, 1:S], ALU.mult, ALU.add))
                step(conv_step, V.scalar_tensor_tensor(y[:, 2:S], u[:, 0:S - 2], tap(0), y[:, 2:S], ALU.mult, ALU.add))
                step(conv_step, V.tensor_tensor(b, b, y, ALU.mult))

            ROUNDS = TOPK // 8
            for t, hh in DOTS:
                add_score(t, hh)
            topk_rounds(2, ROUNDS)
            choose(2)
            convolve(0)
            convolve(1)
            topk_rounds(3, 11)
            convolve(2)
            convolve(3)
            topk_rounds(3, ROUNDS - 11)
            choose(3)
            topk_rounds(4, ROUNDS)
            choose(4)
            for t in range(5, ST):
                topk_rounds(t, ROUNDS)
                choose(t)
            dve.wait_ge(mask_done, ST - 2)

            def q_split(t):
                dve.wait_ge(qs_hi_done, t + 1)
                V.tensor_tensor(qs_lo[:, t % 2], q_raw[:, :, t * P:(t + 1) * P], qs_hi[:, t % 2].bitcast(f32),
                                ALU.subtract).then_inc(qs_lo_done, 1)

            def masked_max(w, a):
                t = w // PT_
                n = (t + 1) * P
                name, cols = logits_of(w, a)
                wait_output(dve, name)
                if w >= 2:
                    wait_output(dve, pt_names(w - 2)[a if wide(w - 2) else 0])
                k = 2 * (w % 2) + a
                ins = V.tensor_tensor_reduce(out=probs[:, w % 2, a, 0:n], in0=psum(name)[:, cols],
                                             in1=mask[:, mask_at(t):mask_at(t + 1)], scale=-scale, scalar=3e38,
                                             op0=ALU.add, op1=ALU.min, accum_out=negmax[:, k:k + 1])
                if wide(w) or a == 1:
                    ins.then_inc(freed(name), 1)
                else:
                    ins.then_inc(first_max_done, 1)

            def probs_lo(name):
                w, src, place = transposed(name)
                dve.wait_ge(pt_hi_done, pt_number[name])
                V.tensor_tensor(place(pt_lo), src, place(pt_hi).bitcast(f32), ALU.subtract).then_inc(freed(name), 1)

            q_split(0)
            for w in range(2):
                for a in range(2):
                    masked_max(w, a)
            for w in range(PAIRS):
                t, p = divmod(w, PT_)
                if p == PT_ - 1:
                    dve.wait_ge(exp_done, NH * (t + 1))
                    if t >= 2:
                        dve.wait_ge(rc_widened, t - 1)
                    V.reciprocal(recips[:, t % 2], sums[:, t % 2]).then_inc(recip_done, 1)
                for a in range(2):
                    if a < len(pt_names(w)):
                        probs_lo(pt_names(w)[a])
                    if w + 2 < PAIRS:
                        masked_max(w + 2, a)
                if p == 0 and t + 1 < ST:
                    q_split(t + 1)
            for p in range(PT_):
                dve.wait_ge(at_hi_done, p + 1)
                V.tensor_tensor(at_lo[:, p], q_raw[:, p], at_hi[:, p].bitcast(f32), ALU.subtract).then_inc(at_lo_done, 1)

            def merge_lo(e):
                dve.wait_ge(mg_hi_done, e + 1)
                V.tensor_tensor(mg_lo[:, e], stage[:, e % 2], mg_hi[:, e].bitcast(f32),
                                ALU.subtract).then_inc(mg_lo_done, 1)

            for e in range(DT):
                wait_output(dve, ("ao", e))
                if e >= 2:
                    dve.wait_ge(mg_lo_done, e - 1)
                dve.wait_ge(gate_loaded[e % 2], 32 * (e // 2 + 1))
                V.tensor_tensor(stage[:, e % 2], psum(("ao", e))[:], gate_in[:, e % 2, 0],
                                ALU.mult).then_inc(freed(("ao", e)), 1)
                wait_evacuated(dve, ("ao", e))
                V.tensor_tensor(stage[:, e % 2], stage[:, e % 2], gate_in[:, e % 2, 1], ALU.add).then_inc(merged, 1)
                if e:
                    merge_lo(e - 1)
            merge_lo(DT - 1)

            def add_to_h(name, e, more=0):
                wait_output(dve, name, more)
                V.tensor_tensor(h[:, e], psum(name)[:], h[:, e], ALU.add).then_inc(freed(name), 1)

            for e in range(DT):
                dve.wait_ge(x_loaded[e], 32)
                add_to_h(("wo", e), e)
                if e:
                    gained_low(1, e - 1, h, T_GFFN, xm_lo(e - 1), xm_hi)
                    accumulate(1, e - 1)
            gained_low(1, DT - 1, h, T_GFFN, xm_lo(DT - 1), xm_hi)
            accumulate(1, DT - 1)
            norm_rms(1)
            wait_evacuated(dve, "n1_bc")
            wait_evacuated(dve, ("up", 0, 0))
            V.tensor_tensor(up_out[:, 0], up_out[:, 0], rrms[1][:], ALU.mult).then_inc(first_up_scaled, 1)

            def conv_taps(g, m, groups, i=None):
                j = 0 if i is None else i
                base_col = T_FCONV + 12 * g + 3 * m

                def tap(k):
                    return const[:, base_col + k:base_col + k + 1] if i is None else const[:, ds(base_col + k + 24 * i, 1)]

                t, src = ff_t[:, m], up_out[:, m % 2]
                if i is not None or g or m:
                    wait_output(dve, ("up", g, m), 24 * j)
                    if i is not None or g or m >= 2:
                        dve.wait_ge(tap0_done, 4 * groups + m - 1)
                    V.tensor_tensor(src, psum(("up", g, m))[:], rrms[1][:], ALU.mult).then_inc(freed(("up", g, m)), 1)
                dve.wait_ge(tap2_done, 4 * groups + m + 1)
                V.scalar_tensor_tensor(t[:, 1:S], src[:, 0:S - 1], tap(1), t[:, 1:S], ALU.mult,
                                       ALU.add).then_inc(tap1_done, 1)
                dve.wait_ge(tap1_done, 4 * groups + m + 1)
                V.scalar_tensor_tensor(t[:, 2:S], src[:, 0:S - 2], tap(0), t[:, 2:S], ALU.mult,
                                       ALU.add).then_inc(tap0_done, 1)

            def gate_times_value(g, a, groups, i=None):
                dve.wait_ge(silu_done, 2 * groups + a + 1)
                dve.wait_ge(tap0_done, 4 * groups + 2 * a + 2)
                V.tensor_tensor(ff_t[:, 2 * a + 1], ff_t[:, 2 * a + 1], stage[:, a], ALU.mult).then_inc(ff_done, 1)

            def ffn_group(g, i=None):
                groups = g if i is None else g + 2 * i
                conv_taps(g, 0, groups, i)
                conv_taps(g, 1, groups, i)
                gate_times_value(g, 0, groups, i)
                conv_taps(g, 2, groups, i)
                conv_taps(g, 3, groups, i)
                gate_times_value(g, 1, groups, i)

            ffn_group(0)
            with dve.Fori(0, 5) as i:
                for n in range(2):
                    ffn_group(1 + n, i)
                    for e in range(DT):
                        add_to_h(("dn", n, e), e, 24 * i)
            for e in range(DT):
                add_to_h(("dn", FT // 2 - 1, e), e)
                if e:
                    accumulate(2, e - 1)
            accumulate(2, DT - 1)
            norm_rms(2)
            wait_evacuated(dve, "n2_bc")
            for d in result_of["dve"]:
                dve.wait_ge(result_gained, d + 1)
                V.tensor_tensor(result[:, d], result[:, d], rrms[1][:],
                                ALU.mult).then_inc(result_scaled["dve"], 1)


def pack(w_in, w_attn_out, w_conv_out, w_o, w_up, w_down):
    def cols(w, c0):
        return w[:, c0:c0 + P].reshape(-1, P, P).transpose(1, 0, 2)

    ikw = np.zeros((D, P), w_in.dtype)
    ikw[:, 0:HD] = w_in[:, IK0:IK0 + HD]
    ikw[:, HD:HD + NH] = w_in[:, IW0:IW0 + NH]
    out = [cols(ikw, 0)]
    out += [cols(w_in, IQ0 + p * P) for p in range(PT_)]
    for p in range(CT):
        out += [cols(w_in, c + p * P) for c in (CH0, CC0, CB0)]

    def two(w, j):
        return np.concatenate([cols(w, (2 * j) * P), cols(w, (2 * j + 1) * P)], axis=1)

    for j in range(4):
        out += [cols(w_in, G0 + D + (2 * j + n) * P) for n in range(2)] + [two(w_conv_out, j)]
    for c in (Q0, K0, V0):
        out += [cols(w_in, c + p * P) for p in range(PT_)]
    out += [cols(w_in, G0 + e * P) for e in range(DT)]
    out += [two(w_attn_out, j) for j in range(4)]
    out += [cols(w_o, e * P) for e in range(DT)]

    def up(g):
        return [cols(w_up, c) for a in range(2) for c in ((2 * g + a) * P, FF + (2 * g + a) * P)]

    def down(g):
        rows = w_down[2 * g * P:(2 * g + 2) * P]
        return [np.concatenate([cols(rows, (4 * n + e) * P) for e in range(4)], axis=1) for n in range(2)]

    out += up(0)
    for g in range(1, FT // 2):
        out += up(g) + down(g - 1)
    out += down(FT // 2 - 1)
    return np.ascontiguousarray(np.stack(out).reshape(N_CHUNKS, P, 8 * P))


def kernel(**inputs):
    import concourse.bacc as bacc
    from concourse.bass_utils import run_bass_kernel_spmd

    a = {k: np.asarray(v) for k, v in inputs.items()}
    x = a["x"]
    xT = np.ascontiguousarray(x[0].T.reshape(DT, P, S))
    wts = pack(a["w_in"][0], a["w_attn_out"][0], a["w_conv_out"][0], a["w_o"][0], a["w_up"][0], a["w_down"][0])

    def per_channel(v):
        return v.reshape(-1, P).T

    fconv = a["ffn_conv_w"][0].reshape(3, 2, FT // 2, 2, P)
    consts = np.ascontiguousarray(np.concatenate([
        per_channel(a["norm_mix_g"][0]), per_channel(a["norm_ffn_g"][0]), per_channel(a["norm_final_g"]),
        per_channel(a["b_gate"][0]), per_channel(a["conv_w"][0].reshape(-1)),
        fconv.transpose(4, 2, 3, 1, 0).reshape(P, -1)], axis=1))
    arrays = {"xT_dram": xT, "wts_dram": wts, "consts_dram": consts}

    nc = bacc.Bacc("TRN2", target_bir_lowering=False, num_devices=1)
    f32 = mybir.dt.float32
    ins = [nc.dram_tensor(n, v.shape, f32, kind="ExternalInput").ap() for n, v in arrays.items()]
    out = nc.dram_tensor("outT_dram", (DT, P, S), f32, kind="ExternalOutput").ap()
    bc_dram = nc.dram_tensor("bc_dram", (DT, P, S), f32, kind="Internal").ap()
    ga_dram = nc.dram_tensor("ga_dram", (DT, P, S), f32, kind="Internal").ap()
    build(nc, *ins, out, bc_dram, ga_dram)
    r = run_bass_kernel_spmd(nc, [arrays], core_ids=[0])
    got = np.asarray(r.results[0]["outT_dram"])
    return np.ascontiguousarray(got.reshape(D, S).T).reshape(x.shape)
```
